# Optimizing a Trainium2 kernel written in Bass

```python
import math
import jax, jax.numpy as jnp
from jax import lax
import numpy as np

D_MODEL = 2048
BATCH = 1
SEQ = 256
DEPTH = 1
DEC_BATCH = 8
DEC_SEQ = 4
PAST_LEN = 2048
PAGE_SIZE = 128

D_MIX = D_MODEL
D_ATTN = D_MIX // 2
D_SSM = D_MIX - D_ATTN
HEAD_DIM = 64
N_HEADS = D_ATTN // HEAD_DIM
N_KV_HEADS = N_HEADS // 4
REP = N_HEADS // N_KV_HEADS
D_KV = N_KV_HEADS * HEAD_DIM
ROT_DIM = HEAD_DIM // 4
ROPE_THETA = 500000.0
WINDOW = 128
Q_BLOCK = 128
SSM_CH = 16
N_SSM_GROUPS = D_SSM // SSM_CH
SSM_STATE = 64
PROJ_COLS = D_ATTN + 2 * D_KV + D_SSM
N_EXPERT_GROUPS = 4
EXPERTS_PER_GROUP = 8
N_EXPERTS = N_EXPERT_GROUPS * EXPERTS_PER_GROUP
D_EXPERT = D_MODEL // 4
TOP_K_IN_GROUP = 2
DEEPNORM_ALPHA = (2.0 * DEPTH) ** 0.25
DEEPNORM_BETA = (8.0 * DEPTH) ** -0.25
LN_EPS = 1e-5

kernel_name = 'hymba_s5_swa_sink_hiermoe_deepnorm_adaln_step'

def _layernorm(x):
    xf = x.astype(jnp.float32)
    mu = jnp.mean(xf, -1, keepdims=True)
    var = jnp.mean(jnp.square(xf - mu), -1, keepdims=True)
    return ((xf - mu) * lax.rsqrt(var + LN_EPS)).astype(x.dtype)

def _rmsnorm(x):
    xf = x.astype(jnp.float32)
    return (xf * lax.rsqrt(jnp.mean(jnp.square(xf), -1, keepdims=True) + LN_EPS)).astype(x.dtype)

def _rotary(x, pos):
    half = ROT_DIM // 2
    inv_freq = ROPE_THETA ** (-jnp.arange(half, dtype=jnp.float32) * 2.0 / ROT_DIM)
    ang = pos.astype(jnp.float32)[:, None] * inv_freq[None, :]
    cos = jnp.cos(ang)[None, :, None, :]
    sin = jnp.sin(ang)[None, :, None, :]
    xr = x[..., :ROT_DIM].astype(jnp.float32)
    x1, x2 = xr[..., :half], xr[..., half:]
    rot = jnp.concatenate([x1 * cos - x2 * sin, x2 * cos + x1 * sin], -1).astype(x.dtype)
    return jnp.concatenate([rot, x[..., ROT_DIM:]], -1)

def _window_attention(q, k_new, v_new, k_prev, v_prev, start, sinks):
    B, L = q.shape[0], q.shape[1]
    qb = Q_BLOCK if L % Q_BLOCK == 0 else L
    nb = L // qb
    k_all = jnp.concatenate([k_prev, k_new], 1)
    v_all = jnp.concatenate([v_prev, v_new], 1)
    k_pos = start - WINDOW + jnp.arange(WINDOW + L)
    q_pos = (start + jnp.arange(L)).reshape(nb, qb)
    kidx = jnp.arange(nb)[:, None] * qb + jnp.arange(qb + WINDOW)[None, :]
    kb = k_all[:, kidx]
    vb = v_all[:, kidx]
    kpb = k_pos[kidx]
    qg = q.reshape(B, nb, qb, N_KV_HEADS, REP, HEAD_DIM)
    s = jnp.einsum('bnqgrd,bnkgd->bgrnqk', qg, kb, preferred_element_type=jnp.float32) * (HEAD_DIM ** -0.5)
    rel = q_pos[:, :, None] - kpb[:, None, :]
    mask = (rel >= 0) & (rel < WINDOW) & (kpb[:, None, :] >= 0)
    s = jnp.where(mask, s, -jnp.inf)
    sink = sinks.astype(jnp.float32).reshape(1, N_KV_HEADS, REP, 1, 1, 1)
    m = jnp.maximum(jnp.max(s, -1, keepdims=True), sink)
    p = jnp.exp(s - m)
    p = p / (jnp.sum(p, -1, keepdims=True) + jnp.exp(sink - m))
    o = jnp.einsum('bgrnqk,bnkgd->bnqgrd', p.astype(vb.dtype), vb)
    return o.reshape(B, L, D_ATTN)

def _complex_affine_combine(e1, e2):
    a1r, a1i, b1r, b1i = e1
    a2r, a2i, b2r, b2i = e2
    return (a2r * a1r - a2i * a1i,
            a2r * a1i + a2i * a1r,
            a2r * b1r - a2i * b1i + b2r,
            a2r * b1i + a2i * b1r + b2i)

def _s5(u, h0_re, h0_im, lam_re, lam_im, log_step, b_re, b_im, c_re, c_im, d_skip):
    B, L = u.shape[0], u.shape[1]
    f32 = jnp.float32
    ug = u.reshape(B, L, N_SSM_GROUPS, SSM_CH).astype(f32)
    dt = jnp.exp(log_step.astype(f32))[:, None]
    lr, li = lam_re.astype(f32), lam_im.astype(f32)
    mag = jnp.exp(lr * dt)
    ar, ai = mag * jnp.cos(li * dt), mag * jnp.sin(li * dt)
    den = lr * lr + li * li
    cr = ((ar - 1.0) * lr + ai * li) / den
    ci = (ai * lr - (ar - 1.0) * li) / den
    br, bi = b_re.astype(f32), b_im.astype(f32)
    bbr = cr[..., None] * br - ci[..., None] * bi
    bbi = cr[..., None] * bi + ci[..., None] * br
    xr = jnp.einsum('gpc,blgc->blgp', bbr, ug)
    xi = jnp.einsum('gpc,blgc->blgp', bbi, ug)
    h0r, h0i = h0_re.astype(f32), h0_im.astype(f32)
    xr = xr.at[:, 0].add(ar * h0r - ai * h0i)
    xi = xi.at[:, 0].add(ar * h0i + ai * h0r)
    a_r = jnp.broadcast_to(ar, xr.shape)
    a_i = jnp.broadcast_to(ai, xi.shape)
    _, _, hr, hi = lax.associative_scan(_complex_affine_combine, (a_r, a_i, xr, xi), axis=1)
    y = (jnp.einsum('gcp,blgp->blgc', c_re.astype(f32), hr)
         - jnp.einsum('gcp,blgp->blgc', c_im.astype(f32), hi)
         + d_skip.astype(f32).reshape(N_SSM_GROUPS, SSM_CH) * ug)
    return y.reshape(B, L, D_SSM).astype(u.dtype), hr[:, -1].astype(h0_re.dtype), hi[:, -1].astype(h0_im.dtype)

def _hier_moe(h, rg_w, rg_b, re_w, re_b, w_gate, w_up, w_down):
    B, L, D = h.shape
    t = h.reshape(B * L, D)
    T = t.shape[0]
    g_logits = jnp.dot(t, rg_w).astype(jnp.float32) + rg_b.astype(jnp.float32)
    g_prob = jax.nn.softmax(g_logits, -1)
    g_val, g_idx = lax.top_k(g_prob, 1)
    e_logits = (jnp.dot(t, re_w).astype(jnp.float32) + re_b.astype(jnp.float32)).reshape(T, N_EXPERT_GROUPS, EXPERTS_PER_GROUP)
    e_in = jnp.take_along_axis(e_logits, g_idx[:, :, None], axis=1)[:, 0]
    e_prob = jax.nn.softmax(e_in, -1)
    e_val, e_idx = lax.top_k(e_prob, TOP_K_IN_GROUP)
    e_val = e_val / jnp.sum(e_val, -1, keepdims=True)
    within = jnp.einsum('tk,tke->te', e_val, jax.nn.one_hot(e_idx, EXPERTS_PER_GROUP, dtype=jnp.float32))
    comb = jax.nn.one_hot(g_idx[:, 0], N_EXPERT_GROUPS, dtype=jnp.float32)[:, :, None] * (g_val * within)[:, None, :]
    comb = comb.reshape(T, N_EXPERTS).astype(h.dtype)
    hg = jnp.einsum('td,edf->tef', t, w_gate)
    hu = jnp.einsum('td,edf->tef', t, w_up)
    act = jax.nn.silu(hg) * hu * comb[:, :, None]
    out = jnp.einsum('tef,efd->td', act, w_down)
    return out.reshape(B, L, D)

def _layer(x, c, start, k_prev, v_prev, h0_re, h0_im, p):
    B, L, _ = x.shape
    mod = jnp.dot(jax.nn.silu(c), p['ada_w']) + p['ada_b']
    sh1, sc1, g1, sh2, sc2, g2 = [m[:, None, :] for m in jnp.split(mod, 6, -1)]
    h = _layernorm(x) * (1.0 + sc1) + sh1
    proj = jnp.dot(h, p['w_in'])
    q, k, v, u = jnp.split(proj, [D_ATTN, D_ATTN + D_KV, D_ATTN + 2 * D_KV], -1)
    pos = start + jnp.arange(L)
    q = _rotary(q.reshape(B, L, N_HEADS, HEAD_DIM), pos)
    k = _rotary(k.reshape(B, L, N_KV_HEADS, HEAD_DIM), pos)
    v = v.reshape(B, L, N_KV_HEADS, HEAD_DIM)
    attn = _window_attention(q, k, v, k_prev, v_prev, start, p['attn_sinks'])
    y_ssm, hr, hi = _s5(u, h0_re, h0_im, p['ssm_lambda_re'], p['ssm_lambda_im'], p['ssm_log_step'],
                        p['ssm_b_re'], p['ssm_b_im'], p['ssm_c_re'], p['ssm_c_im'], p['ssm_d'])
    z = jax.nn.gelu(y_ssm)
    ssm = z * jax.nn.sigmoid(jnp.dot(z, p['ssm_glu_w']) + p['ssm_glu_b'])
    mixed = jnp.concatenate([_rmsnorm(attn) * p['attn_norm_g'], _rmsnorm(ssm) * p['ssm_norm_g']], -1)
    o = jnp.dot(mixed, p['w_out'])
    x = _layernorm(DEEPNORM_ALPHA * x + g1 * o) * p['ln1_g'] + p['ln1_b']
    h2 = _layernorm(x) * (1.0 + sc2) + sh2
    f = _hier_moe(h2, p['router_group_w'], p['router_group_b'], p['router_expert_w'], p['router_expert_b'],
                  p['exp_w_gate'], p['exp_w_up'], p['exp_w_down'])
    x = _layernorm(DEEPNORM_ALPHA * x + g2 * f) * p['ln2_g'] + p['ln2_b']
    k_buf = jnp.concatenate([k_prev, k], 1)[:, -WINDOW:]
    v_buf = jnp.concatenate([v_prev, v], 1)[:, -WINDOW:]
    return x, k_buf, v_buf, hr, hi

def setup_inputs(seed: int = 0) -> dict:
    key = jax.random.key(seed)
    ks = iter(jax.random.split(key, 48))
    f32 = jnp.float32

    def nrm(shape, scale=1.0):
        return jax.random.normal(next(ks), shape, f32) * scale

    L = DEPTH
    n_idx = jnp.arange(SSM_STATE, dtype=f32)
    inp = {}
    inp['x_prompt'] = nrm((BATCH, SEQ, D_MODEL))
    inp['x_sample'] = nrm((DEC_BATCH, DEC_SEQ, D_MODEL))
    inp['cache_k_win'] = nrm((L, DEC_BATCH, WINDOW, N_KV_HEADS, HEAD_DIM))
    inp['cache_v_win'] = nrm((L, DEC_BATCH, WINDOW, N_KV_HEADS, HEAD_DIM))
    inp['state_ssm_re'] = nrm((L, DEC_BATCH, N_SSM_GROUPS, SSM_STATE), 0.1)
    inp['state_ssm_im'] = nrm((L, DEC_BATCH, N_SSM_GROUPS, SSM_STATE), 0.1)
    inp['c_prompt'] = nrm((BATCH, D_MODEL))
    inp['c_sample'] = nrm((DEC_BATCH, D_MODEL))
    inp['ada_w'] = nrm((L, D_MODEL, 6 * D_MODEL), 0.5 * D_MODEL ** -0.5)
    inp['ada_b'] = nrm((L, 6 * D_MODEL), 0.01)
    inp['w_in'] = nrm((L, D_MODEL, PROJ_COLS), D_MODEL ** -0.5)
    inp['attn_sinks'] = nrm((L, N_HEADS), 0.5)
    inp['ssm_lambda_re'] = -0.5 + nrm((L, N_SSM_GROUPS, SSM_STATE), 0.01)
    inp['ssm_lambda_im'] = math.pi * n_idx + nrm((L, N_SSM_GROUPS, SSM_STATE), 0.01)
    inp['ssm_log_step'] = jax.random.uniform(next(ks), (L, N_SSM_GROUPS), f32, math.log(1e-3), math.log(1e-1))
    inp['ssm_b_re'] = nrm((L, N_SSM_GROUPS, SSM_STATE, SSM_CH), (2 * SSM_CH) ** -0.5)
    inp['ssm_b_im'] = nrm((L, N_SSM_GROUPS, SSM_STATE, SSM_CH), (2 * SSM_CH) ** -0.5)
    inp['ssm_c_re'] = nrm((L, N_SSM_GROUPS, SSM_CH, SSM_STATE), SSM_STATE ** -0.5)
    inp['ssm_c_im'] = nrm((L, N_SSM_GROUPS, SSM_CH, SSM_STATE), SSM_STATE ** -0.5)
    inp['ssm_d'] = nrm((L, D_SSM))
    inp['ssm_glu_w'] = nrm((L, D_SSM, D_SSM), D_SSM ** -0.5)
    inp['ssm_glu_b'] = nrm((L, D_SSM), 0.01)
    inp['attn_norm_g'] = 1.0 + nrm((L, D_ATTN), 0.01)
    inp['ssm_norm_g'] = 1.0 + nrm((L, D_SSM), 0.01)
    inp['w_out'] = nrm((L, D_MIX, D_MODEL), D_MIX ** -0.5 * DEEPNORM_BETA)
    inp['ln1_g'] = 1.0 + nrm((L, D_MODEL), 0.01)
    inp['ln1_b'] = nrm((L, D_MODEL), 0.01)
    inp['router_group_w'] = nrm((L, D_MODEL, N_EXPERT_GROUPS), D_MODEL ** -0.5)
    inp['router_group_b'] = nrm((L, N_EXPERT_GROUPS), 0.01)
    inp['router_expert_w'] = nrm((L, D_MODEL, N_EXPERTS), D_MODEL ** -0.5)
    inp['router_expert_b'] = nrm((L, N_EXPERTS), 0.01)
    inp['exp_w_gate'] = nrm((L, N_EXPERTS, D_MODEL, D_EXPERT), D_MODEL ** -0.5)
    inp['exp_w_up'] = nrm((L, N_EXPERTS, D_MODEL, D_EXPERT), D_MODEL ** -0.5)
    inp['exp_w_down'] = nrm((L, N_EXPERTS, D_EXPERT, D_MODEL), D_EXPERT ** -0.5 * DEEPNORM_BETA)
    inp['ln2_g'] = 1.0 + nrm((L, D_MODEL), 0.01)
    inp['ln2_b'] = nrm((L, D_MODEL), 0.01)
    return inp

def reference(x_prompt, x_sample, cache_k_win, cache_v_win, state_ssm_re, state_ssm_im, c_prompt, c_sample,
              ada_w, ada_b, w_in, attn_sinks, ssm_lambda_re, ssm_lambda_im, ssm_log_step, ssm_b_re, ssm_b_im,
              ssm_c_re, ssm_c_im, ssm_d, ssm_glu_w, ssm_glu_b, attn_norm_g, ssm_norm_g, w_out, ln1_g, ln1_b,
              router_group_w, router_group_b, router_expert_w, router_expert_b, exp_w_gate, exp_w_up, exp_w_down,
              ln2_g, ln2_b):
    y_prompt, y_sample = x_prompt, x_sample
    bp = x_prompt.shape[0]
    kp_l, vp_l, hrp_l, hip_l = [], [], [], []
    ks_l, vs_l, hrs_l, his_l = [], [], [], []
    for l in range(DEPTH):
        p = dict(ada_w=ada_w[l], ada_b=ada_b[l], w_in=w_in[l], attn_sinks=attn_sinks[l],
                 ssm_lambda_re=ssm_lambda_re[l], ssm_lambda_im=ssm_lambda_im[l], ssm_log_step=ssm_log_step[l],
                 ssm_b_re=ssm_b_re[l], ssm_b_im=ssm_b_im[l], ssm_c_re=ssm_c_re[l], ssm_c_im=ssm_c_im[l],
                 ssm_d=ssm_d[l], ssm_glu_w=ssm_glu_w[l], ssm_glu_b=ssm_glu_b[l],
                 attn_norm_g=attn_norm_g[l], ssm_norm_g=ssm_norm_g[l], w_out=w_out[l],
                 ln1_g=ln1_g[l], ln1_b=ln1_b[l], router_group_w=router_group_w[l], router_group_b=router_group_b[l],
                 router_expert_w=router_expert_w[l], router_expert_b=router_expert_b[l],
                 exp_w_gate=exp_w_gate[l], exp_w_up=exp_w_up[l], exp_w_down=exp_w_down[l],
                 ln2_g=ln2_g[l], ln2_b=ln2_b[l])
        k0 = jnp.zeros((bp, WINDOW, N_KV_HEADS, HEAD_DIM), x_prompt.dtype)
        h0 = jnp.zeros((bp, N_SSM_GROUPS, SSM_STATE), state_ssm_re.dtype)
        y_prompt, kp, vp, hrp, hip = _layer(y_prompt, c_prompt, 0, k0, k0, h0, h0, p)
        y_sample, ksm, vsm, hrs, his = _layer(y_sample, c_sample, PAST_LEN, cache_k_win[l], cache_v_win[l],
                                              state_ssm_re[l], state_ssm_im[l], p)
        kp_l.append(kp); vp_l.append(vp); hrp_l.append(hrp); hip_l.append(hip)
        ks_l.append(ksm); vs_l.append(vsm); hrs_l.append(hrs); his_l.append(his)
    k_win_prompt = jnp.stack(kp_l)
    v_win_prompt = jnp.stack(vp_l)
    ssm_re_prompt = jnp.stack(hrp_l)
    ssm_im_prompt = jnp.stack(hip_l)
    k_win_sample = jnp.stack(ks_l)
    v_win_sample = jnp.stack(vs_l)
    ssm_re_sample = jnp.stack(hrs_l)
    ssm_im_sample = jnp.stack(his_l)
    return (y_prompt, y_sample, k_win_prompt, v_win_prompt, ssm_re_prompt, ssm_im_prompt,
            k_win_sample, v_win_sample, ssm_re_sample, ssm_im_sample)


_drawn_inputs = setup_inputs


def setup_inputs(seed=0):
    import zlib

    import numpy as np

    out = dict(_drawn_inputs(seed))
    spreads = {}
    factors = {'ada_b': 2.689,
     'attn_sinks': 8.0,
     'ssm_lambda_re': 17.004,
     'ssm_c_re': 5.826,
     'ssm_c_im': 5.745,
     'ssm_glu_b': 23.504,
     'attn_norm_g': 64.0,
     'ssm_norm_g': 64.0,
     'ln1_g': 28.434,
     'ln1_b': 30.413,
     'router_group_b': 64.0,
     'router_expert_b': 64.0,
     'ln2_g': 32.802,
     'ln2_b': 33.301,
     'router_group_w': 7.581,
     'router_expert_w': 7.778,
     'exp_w_gate': 7.312,
     'exp_w_up': 6.895,
     'exp_w_down': 6.771}
    for name, (base, spread) in spreads.items():
        noise = np.random.default_rng([zlib.crc32(name.encode()), seed]).standard_normal(out[name].shape)
        drawn = base * np.exp(spread * noise) if base else spread * noise
        out[name] = __import__('jax').numpy.asarray(drawn.astype(out[name].dtype))
    for name, factor in factors.items():
        out[name] = (out[name] * factor).astype(out[name].dtype)
    return out
```

```python
from contextlib import ExitStack

import numpy as np
import concourse.bass as bass
from concourse import mybir

F32 = mybir.dt.float32
I32 = mybir.dt.int32
ALU = mybir.AluOpType
ACT = mybir.ActivationFunctionType
AX = mybir.AxisListType

P = 128
D = 2048
KD = D // P
SEQ, NB, DS = 256, 8, 4
NS = NB * DS
T = SEQ + NS
BLK = [(0, 128), (1, 128), (2, NS)]
WIN = 128
HD, NH, NKV, REP = 64, 16, 4, 4
DA, DKV, DSSM = 1024, 256, 1024
QKV = DA + 2 * DKV
G, CH, ST = 64, 16, 64
NP = G // 2
E, EPG, NEG, FE = 32, 8, 4, 512
SLOTS = 64
XB = 2 * T // (SLOTS + 1)
NBLK = E + XB
EPS = 1e-5
ALPHA = 2.0 ** 0.25
BIG = 1e30
NROW = 9

PRE_RING = 6
RING = 12
ADA_STEPS = 3
WARM = 5
LN_DONE = {"ln_in": 0, "ln1": 3, "ln0": 6, "ln2": 9}
TURN = [6.28125, float(np.float32(round((2 * np.pi - 6.28125) * 2 ** 20) / 2 ** 20))]
TURN.append(2 * np.pi - TURN[0] - TURN[1])
PI_IN = 3.1415925

C_ID, C_ONE, C_IOTA, C_ROT, C_SEL, C_N = 0, 128, 256, 320, 368, 528
R_LT, R_E, R_VAL, R_K, R_OUT, R_J = 0, 128, 160, 163, 171, 174
R_N = R_J + NBLK
M_PREV, M_SELF, M_CACHE, M_NEW, M_N = 0, 128, 256, 384, 640
I_EXPERT, I_FIRST, I_N = 1, 1 + NBLK, 1 + NBLK + E


def constants():
    c = np.zeros((P, C_N), np.float32)
    i = np.arange(P)
    c[:, C_ID:C_ID + P] = np.eye(P)
    c[:, C_ONE:C_ONE + P] = 1.0
    c[:, C_IOTA:C_IOTA + SLOTS] = np.arange(SLOTS)
    inv = (np.float32(500000.0) ** (-np.arange(8, dtype=np.float32) * np.float32(2.0) / np.float32(16))).astype(np.float32)
    for b, n in BLK:
        pos = i + b * P if b < 2 else 2048 + i % DS
        ang = (pos.astype(np.float32)[:, None] * inv[None, :]).astype(np.float32)
        c[:, C_ROT + 16 * b:C_ROT + 16 * b + 8] = np.cos(ang.astype(np.float64))
        c[:, C_ROT + 16 * b + 8:C_ROT + 16 * b + 16] = np.sin(ang.astype(np.float64))
    for g in range(4):
        c[32 * g, C_SEL:C_SEL + P] = 1.0
        for b in range(NB):
            c[32 * g + 1 + b, C_SEL + P + DS * b:C_SEL + P + DS * b + DS] = 1.0
    r = np.zeros((P, R_N), np.float32)
    r[:, R_LT:R_LT + P] = i[:, None] < i[None, :]
    r[:, R_E:R_E + E] = np.arange(E)
    r[:, R_VAL:R_VAL + 3] = 1.0
    r[NS:, R_VAL + 2] = 0.0
    r[NS:, R_OUT + 2] = 1.0
    r[:, R_K:R_K + 8] = np.arange(8, 0, -1)
    r[:, R_J:R_J + NBLK] = np.arange(NBLK)
    m = np.zeros((P, M_N), np.float32)
    m[:, M_PREV:M_PREV + P] = np.where(i[None, :] > i[:, None], 0.0, -BIG)
    m[:, M_SELF:M_SELF + P] = np.where(i[None, :] <= i[:, None], 0.0, -BIG)
    t = (i % DS)[:, None]
    m[:, M_CACHE:M_CACHE + P] = np.where(i[None, :] > t, 0.0, -BIG)
    for b in range(NB):
        j = np.arange(NS)[None, :]
        m[:, M_NEW + NS * b:M_NEW + NS * b + NS] = np.where((j // DS == b) & (j % DS <= t), 0.0, -BIG)
    return c, m, r


def chunk_plan():
    plan = [("ada", v, k) for v in (0, 1) for k in range(KD)]
    plan += [("u", i, 0) for i in range(8)]
    for j in range(NP // 2):
        plan += [("ada", 2 + s // KD, s % KD) for s in range(ADA_STEPS * j, ADA_STEPS * (j + 1))]
        plan += [("qkv", j // 4, j % 4)] if j < 12 else []
    plan += [("ada", 5, k) for k in range(KD)]
    plan += [("glu", i, 0) for i in range(4)]
    plan += [("out", h, i) for h in range(2) for i in range(8)]
    return plan


def pt_count(i):
    return sum(1 if u < NKV else 2 for u in range(i))


def spread(ap, n):
    return ap.unsqueeze(len(ap.shape)).to_broadcast(list(ap.shape) + [n])


def spread_mid(ap, n):
    return ap.unsqueeze(1).to_broadcast([ap.shape[0], n, ap.shape[1]])


def build(nc, a, o, scratch):
    plan = chunk_plan()
    first = {}
    for n, c in enumerate(plan):
        first.setdefault(c, n)
    last_slot_uses = [len([n for n in range(len(plan)) if n % PRE_RING == s]) if s < PRE_RING else 0
                      for s in range(RING)]
    n_a, n_b, n_c = first[("u", 0, 0)], first[("ada", 5, 0)], first[("glu", 0, 0)]
    attn_dram, y_dram = scratch

    with ExitStack() as ctx:
        def sb(name, shape, dt=F32):
            return ctx.enter_context(nc.sbuf_tensor(name, shape, dt))

        ring = sb("ring", [P, RING, 2048])
        X = sb("X", [P, 3, D])
        H = sb("H", [P, 3, D])
        MT = sb("MT", [P, KD, T])
        MOD = sb("MOD", [P, 4, 512])
        GE = sb("GE", [P, 2, D])
        BC = sb("BC", [P, 4, 8, P])
        con = sb("con", [P, C_N])
        cT = sb("cT", [P, KD, 32])
        st = sb("st", [P, 3, 32])
        vT = sb("vT", [P, 32])
        HF = sb("HF", [P, 2, NP])
        slot_f = sb("slot_f", [P, 3, 2])
        slot_i = sb("slot_i", [P, 3, 2], I32)
        sink = sb("sink", [P, NH])
        sinkc = sb("sinkc", [P, 1])
        mx, smx, nm, den, esink, rd = (sb(n, [P, REP]) for n in ("mx", "smx", "nm", "den", "esink", "rd"))
        smxx, ssmx, snm, sden, sesink = (sb(n, [P, NB]) for n in ("smxx", "ssmx", "snm", "sden", "sesink"))
        ssq, rms = sb("ssq", [P, 3]), sb("rms", [P, 3])
        cwt = sb("cwt", [P, 3, 2])
        rint = sb("rint", [1, I_N], I32)
        bank = ctx.enter_context(nc.psum_tensor("bank", [P, 8, 512], F32))

        ident = con[:, C_ID:C_ID + P]
        ones = con[:, C_ONE:C_ONE + P]
        later = ring[:, 6:12, :].rearrange("p a b -> p (a b)")
        Hf = H[:, :, :].rearrange("p a b -> p (a b)")
        Xf = X[:, :, :].rearrange("p a b -> p (a b)")
        GEf = GE[:, :, :].rearrange("p a b -> p (a b)")
        BCf = BC[:, :, :, :].rearrange("p a b c -> p (a b c)")
        co = Hf[:, 5888:5888 + 7 * NP].rearrange("p (i q) -> p i q", i=7)
        tab = ring[:, 6:8, :].rearrange("p b (c q t) -> p b c q t", c=2, q=4)
        KC = ring[:, 8, :].rearrange("p (b d) -> p b d", b=NB)
        VC = ring[:, 9, :].rearrange("p (b d) -> p b d", b=NB)
        kcT = ring[:, 10, :].rearrange("p (b g w) -> p b g w", b=NB, g=2)
        XS = ring[:, 11, :].rearrange("p (q c b t) -> p q c b t", q=NP, c=2, b=NB)
        XSf = ring[:, 11, :].rearrange("p (q c n) -> p q c n", q=NP, c=2)
        UT = Hf[:, 3584:3584 + 8 * T].rearrange("p (m t) -> p m t", m=8)
        Wk = Hf[:, 0:3584].rearrange("p (n t) -> p n t", n=14)
        qkv = Xf[:, 0:3 * QKV].rearrange("p (b n) -> p b n", b=3)
        Pb = Xf[:, 4608:5632].rearrange("p (h w) -> p h w", h=4)
        QS = Xf[:, 5632:6144].rearrange("p (b g r) -> p b g r", b=NB, g=2)
        TBa = GEf[:, 0:1024].rearrange("p (i q t) -> p i q t", i=2, q=4)
        crow = GEf[0:NROW, 0:2048]
        mod01 = GEf[:, 2048:3072].rearrange("p (v n) -> p v n", v=2)
        modT = GEf[:, 3072:3072 + 288].rearrange("p (v k r) -> p v k r", v=2, k=KD)
        H0 = GEf[:, 3360:3872].rearrange("p (c b q) -> p c b q", c=2, b=NB)
        QT = GEf[:, 0:8 * T].rearrange("p (i t) -> p i t", i=8)
        mask = GEf[:, 2304:2304 + M_N]
        PT = GEf[:, 2944:3968].rearrange("p (j h q) -> p j h q", j=2, h=4)
        KT = MT[:, 8:10, :]
        BT = [BC[:, 0, :, :], BC[:, 1, :, :]]
        CT = [BC[:, 2, :, :], BC[:, 3, :, :]]

        sems = {}

        def S(name):
            if name not in sems:
                sems[name] = ctx.enter_context(nc.semaphore(name))
            return sems[name]

        landed = [S(f"landed{i}") for i in range(RING)]
        used = S("used")

        class Chain:

            def __init__(self, s):
                self.s, self.n = s, 0

            def tick(self, ins):
                self.n += 1
                ins.then_inc(self.s, 1)

            def settle(self, eng):
                eng.wait_ge(self.s, self.n)

        dve_chain, pool_chain = Chain(S("dve_self")), Chain(S("pool_self"))

        ada = a["ada_w"][0].rearrange("(p k) n -> p k n", k=KD)
        win = a["w_in"][0].rearrange("(p k) n -> p k n", k=KD)
        glu = a["ssm_glu_w"][0].rearrange("(i m p) n -> i p m n", m=2, p=P)
        wout = a["w_out"][0].rearrange("(i m p) n -> i p m n", m=2, p=P)

        def load_chunks(sp, begin, end):
            for n in range(begin, min(end, len(plan))):
                kind, v, k = plan[n]
                slot = n % PRE_RING
                if n >= PRE_RING:
                    sp.wait_ge(used, n - PRE_RING + 1)
                dst = ring[:, slot, :]
                if kind == "ada":
                    src = ada[:, k, v * D:(v + 1) * D]
                elif kind == "u":
                    dst, src = dst.rearrange("p (k n) -> p k n", k=2), win[:, 2 * v:2 * v + 2, QKV:QKV + DSSM]
                elif kind == "qkv":
                    dst, src = dst.rearrange("p (k n) -> p k n", k=4), win[:, 4 * k:4 * k + 4, 512 * v:512 * v + 512]
                elif kind == "glu":
                    dst, src = dst.rearrange("p (m n) -> p m n", m=2), glu[v]
                else:
                    dst, src = dst.rearrange("p (m n) -> p m n", m=2), wout[k][:, :, 1024 * v:1024 * v + 1024]
                sp.dma_start(dst, src).then_inc(landed[slot], 16)

        def arrived(pe, n):
            pe.wait_ge(landed[n % PRE_RING], 16 * (n // PRE_RING + 1))
            return ring[:, n % PRE_RING, :]

        def ada_step(pe, v, k, b):
            w = arrived(pe, first[("ada", v, k)])
            for g in range(4):
                mm = pe.matmul(bank[32 * g:32 * g + 32, b, :], cT[:, k, :], w[:, 512 * g:512 * g + 512],
                               start=(k == 0), stop=(k == KD - 1))
            return mm.then_inc(used, 1)

        def ln_stats(dve, src, key):
            for b, n in BLK:
                for c in range(4):
                    dve_chain.tick(nc.vector.bn_stats(st[0:n, b, 6 * c:6 * c + 6], src[0:n, b, 512 * c:512 * c + 512]))
            dve_chain.settle(dve)
            ln_finish(dve, key)

        def ln_finish(dve, key):
            for b, n in BLK:
                dve_chain.tick(nc.vector.bn_aggr(st[0:n, b, 24:26], st[0:n, b, 0:24].rearrange("p (c s) -> p c s", c=4)))
            dve_chain.settle(dve)
            for b, n in BLK:
                nc.vector.tensor_scalar(st[0:n, b, 26:27], st[0:n, b, 25:26], EPS, None, ALU.add)                  .then_inc(S("ln_var"), 1)
            dve.wait_ge(S("ln_std"), LN_DONE[key] + 3)
            for b, n in BLK:
                dve_chain.tick(nc.vector.reciprocal(st[0:n, b, 28:29], st[0:n, b, 27:28]))
            dve_chain.settle(dve)

        def ln_sqrt_of(act, key, b, n):
            act.wait_ge(S("ln_var"), LN_DONE[key] + b + 1)
            nc.scalar.activation(st[0:n, b, 27:28], st[0:n, b, 26:27], ACT.Sqrt).then_inc(S("ln_std"), 1)

        def ln_sqrt(act, key):
            for b, n in BLK:
                ln_sqrt_of(act, key, b, n)

        def ln_scale(dst, src, b, n):
            return nc.vector.tensor_scalar(dst[0:n, b, :], src[0:n, b, :], st[0:n, b, 24:25], st[0:n, b, 28:29],
                                           ALU.subtract, ALU.mult)

        def load_expert_chunk(sp, e, j):
            if j < 8:
                w = a["exp_w_up" if j % 2 else "exp_w_gate"][0].rearrange("e (p k) f -> e p (k f)", k=KD)
                src = w[bass.ds(e, 1), :, 2048 * (j // 2):2048 * (j // 2) + 2048]
            else:
                w = a["exp_w_down"][0].rearrange("e (p j) d -> e p (j d)", j=4)
                src = w[bass.ds(e, 1), :, D * (j - 8):D * (j - 8) + D]
            sp.dma_start(ring[:, j, :], src.rearrange("o p n -> (o p) n")).then_inc(landed[j], 16)

        Bw = Hf[:, 0:2048].rearrange("p (c q n) -> p c q n", c=2, q=NP)
        Cw = Hf[:, 2048:4096].rearrange("p (c m n) -> p c m n", c=2, m=8)
        Braw = later[:, 4096:5120].rearrange("p (c q n) -> p c q n", c=2, q=NP)
        tmpB = later[:, 5120:7168].rearrange("p (i q n) -> p i q n", i=4, q=NP)
        lam = later[0:NP, 7168:7424].rearrange("p (c n) -> p c n", c=2)
        lstep = later[0:NP, 7424:7426]
        dt2 = later[0:NP, 7426:7428]
        cw = later[0:NP, 7680:9728].rearrange("p (i n) -> p i n", i=16)
        srow = later[:, 9728:10240].rearrange("p (j c n) -> p j c n", j=2, c=2)
        vrow = later[0:32, 10240:10368]
        MAG, COS, SIN, CR, CI, AR, AI, TH, RR, R2, T1, T2, T3, DEN, A1, KK = range(16)

        def rotations(dve, j, tmp):
            V = nc.vector

            def tt(dst, x, y, o):
                dve_chain.tick(V.tensor_tensor(dst, x, y, o))

            c, s = tab[:, j % 2, 0, :, :], tab[:, j % 2, 1, :, :]
            dve_chain.tick(V.tensor_copy(c[:, :, 0], co[:, COS, 4 * j:4 * j + 4]))
            dve_chain.tick(V.tensor_copy(s[:, :, 0], co[:, SIN, 4 * j:4 * j + 4]))
            dve_chain.settle(dve)
            n = 1
            while n < SEQ:
                pc, ps = spread(c[:, :, n - 1], n), spread(s[:, :, n - 1], n)
                lo, hi = slice(0, n), slice(n, 2 * n)
                tt(tmp[:, 0, :, lo], c[:, :, lo], pc, ALU.mult), tt(c[:, :, hi], s[:, :, lo], ps, ALU.mult)
                tt(tmp[:, 1, :, lo], s[:, :, lo], pc, ALU.mult), tt(s[:, :, hi], c[:, :, lo], ps, ALU.mult)
                dve_chain.settle(dve)
                tt(c[:, :, hi], tmp[:, 0, :, lo], c[:, :, hi], ALU.subtract)
                tt(s[:, :, hi], tmp[:, 1, :, lo], s[:, :, hi], ALU.add)
                dve_chain.settle(dve)
                n *= 2

        with nc.Block() as block:
            @block.sync
            def _(sp):
                load_chunks(sp, 0, n_a + PRE_RING)

            @block.gpsimd
            def _(pool):
                for i, s in ((0, "ssm_lambda_re"), (1, "ssm_lambda_im")):
                    pool.dma_start(lam[:, i, :], a[s][0].rearrange("(q h) n -> q (h n)", h=2)).then_inc(S("lam_in"), 16)
                pool.dma_start(lstep, a["ssm_log_step"][0].rearrange("(q h) -> q h", h=2)).then_inc(S("lam_in"), 16)
                pool_chain.tick(nc.gpsimd.memset(Bw[:, :, :, :], 0.0))
                pool_chain.tick(nc.gpsimd.memset(Cw[:, :, :, :], 0.0))
                pool_chain.settle(pool)
                for i, s in ((0, "ssm_b_re"), (1, "ssm_b_im")):
                    for h in range(2):
                        pool.dma_start(Braw[64 * h:64 * h + 64, i, :, :],
                                       a[s][0].rearrange("(q h) n c -> h n q c", h=2)[h]).then_inc(S("b_in"), 16)
                for i, s in ((0, "ssm_c_re"), (1, "ssm_c_im")):
                    for q in range(4):
                        for h in range(2):
                            r = 32 * q + 16 * h
                            pool.dma_start(Cw[r:r + 16, i, :, 64 * h:64 * h + 64],
                                           a[s][0].rearrange("(m q h) c n -> q h c m n", q=4, h=2)[q, h])\
                                .then_inc(S("c_in"), 16)
                for i, s in ((0, "state_ssm_re"), (1, "state_ssm_im")):
                    pool.dma_start(srow[:, :, i, :], a[s][0].rearrange("(j b) (q h) n -> (b q) j (h n)", j=2, h=2))\
                        .then_inc(S("state_in"), 16)
                for i, s in enumerate(("attn_norm_g", "ssm_norm_g", "ssm_glu_b", "ssm_d")):
                    pool.dma_start(vrow[8 * i:8 * i + 8, :], a[s][0].rearrange("(m p) -> m p", p=P))\
                        .then_inc(S("vec_in"), 16)
                pool.wait_ge(S("co_ready"), 1)
                pool.wait_ge(S("b_in"), 64)
                crb, cib = spread(co[:, CR, :], CH), spread(co[:, CI, :], CH)
                for i, (c, x) in enumerate(((crb, 0), (cib, 1), (crb, 1), (cib, 0))):
                    pool_chain.tick(nc.gpsimd.tensor_tensor(tmpB[:, i, :, :], c, Braw[:, x, :, :], ALU.mult))
                pool_chain.settle(pool)
                for h in range(2):
                    r, c = slice(64 * h, 64 * h + 64), slice(16 * h, 16 * h + 16)
                    nc.gpsimd.tensor_tensor(Bw[r, 0, :, c], tmpB[r, 0, :, :], tmpB[r, 1, :, :], ALU.subtract)\
                      .then_inc(S("bw_ready"), 1)
                    nc.gpsimd.tensor_tensor(Bw[r, 1, :, c], tmpB[r, 2, :, :], tmpB[r, 3, :, :], ALU.add)\
                      .then_inc(S("bw_ready"), 1)

            @block.scalar
            def _(act):
                act.dma_start(con[:, :], a["consts"]).then_inc(S("con_in"), 16)
                act.dma_start(crow[0:1, :], a["c_prompt"]).then_inc(S("cond_in"), 16)
                act.dma_start(crow[1:NROW, :], a["c_sample"]).then_inc(S("cond_in"), 16)
                act.dma_start(X[:, 0:2, :], a["x_prompt"][0].rearrange("(b p) d -> p b d", b=2)).then_inc(S("x_in"), 16)
                act.dma_start(X[0:NS, 2, :], a["x_sample"].rearrange("b t d -> (b t) d")).then_inc(S("x_in"), 16)
                for g in range(4):
                    ab = a["ada_b"].rearrange("o (v g n) -> g o v n", v=6, g=4)[g]
                    act.dma_start(mod01[32 * g:32 * g + 32, :, :], ab[:, 0:2, :].to_broadcast([32, 2, 512]))\
                       .then_inc(S("adab_in"), 16)
                    act.dma_start(MOD[32 * g:32 * g + 32, :, :], ab[:, 2:6, :].to_broadcast([32, 4, 512]))\
                       .then_inc(S("adab_in"), 16)
                act.wait_ge(S("cond_in"), 32)
                nc.scalar.activation(crow, crow, ACT.Silu).then_inc(S("silu_c"), 1)
                act.wait_ge(S("lam_in"), 48)
                nc.scalar.activation(dt2, lstep, ACT.Exp).then_inc(S("dt_ready"), 1)
                act.wait_ge(S("decay_ready"), 1)
                nc.scalar.activation(cw[:, MAG, :], cw[:, T1, :], ACT.Exp).then_inc(S("mag_ready"), 1)
                act.wait_ge(S("angle_ready"), 1)
                nc.scalar.activation(cw[:, SIN, :], cw[:, RR, :], ACT.Sin).then_inc(S("trig_ready"), 1)
                act.wait_ge(S("angle_ready"), 2)
                nc.scalar.activation(cw[:, COS, :], cw[:, R2, :], ACT.Sin).then_inc(S("trig_ready"), 1)
                ln_sqrt(act, "ln_in")
                for i in range(12):
                    b, n = BLK[i // 4]
                    act.wait_ge(S("xt_ps"), i + 1)
                    nc.scalar.copy(MT[:, 4 * (i % 4):4 * (i % 4) + 4, P * b:P * b + n],
                                   bank[:, 2 + i % 2, 0:4 * n].rearrange("p (k t) -> p k t", k=4))\
                      .then_inc(S("xt_ready"), 1)
                for i in range(8):
                    act.wait_ge(S("bct_ps"), i + 1)
                    w, m = i // 2, 4 * (i % 2)
                    dst = (BT + CT)[w][:, m:m + 4, :]
                    nc.scalar.mul(dst, bank[:, 4 + i % 2, :].rearrange("p (m n) -> p m n", m=4), -1.0 if w == 3 else 1.0)\
                      .then_inc(S("bct_ready"), 1)

            @block.vector
            def _(dve):
                V = nc.vector
                dve_chain.tick(V.memset(cT[:, :, :], 0.0))
                dve_chain.settle(dve)
                dve.wait_ge(S("ct_ps"), 1)
                V.tensor_copy(cT[:, :, 0:NROW], bank[:, 7, 0:KD * NROW].rearrange("p (k r) -> p k r", k=KD))\
                 .then_inc(S("ct_ready"), 1)
                dve.wait_ge(S("x_in"), 32)
                dve.wait_ge(S("dt_ready"), 1)
                dt = spread(dt2, ST)
                dve_chain.tick(V.tensor_tensor(cw[:, T1, :].rearrange("p (h n) -> p h n", h=2),
                                               lam[:, 0, :].rearrange("p (h n) -> p h n", h=2), dt, ALU.mult))
                dve_chain.settle(dve)
                V.tensor_tensor(cw[:, TH, :].rearrange("p (h n) -> p h n", h=2),
                                lam[:, 1, :].rearrange("p (h n) -> p h n", h=2), dt, ALU.mult)\
                 .then_inc(S("decay_ready"), 1)
                dve.wait_ge(S("decay_ready"), 1)
                steps = [
                    lambda: V.tensor_scalar(cw[:, KK, :], cw[:, TH, :], 1.0 / (2 * np.pi), 12582912.0, ALU.mult, ALU.add),
                    lambda: V.tensor_scalar(cw[:, KK, :], cw[:, KK, :], 12582912.0, None, ALU.subtract),
                    lambda: V.scalar_tensor_tensor(out=cw[:, RR, :], in0=cw[:, KK, :], scalar=-TURN[0], in1=cw[:, TH, :],
                                                   op0=ALU.mult, op1=ALU.add),
                    lambda: V.scalar_tensor_tensor(out=cw[:, RR, :], in0=cw[:, KK, :], scalar=-TURN[1], in1=cw[:, RR, :],
                                                   op0=ALU.mult, op1=ALU.add),
                    lambda: V.scalar_tensor_tensor(out=cw[:, RR, :], in0=cw[:, KK, :], scalar=-TURN[2], in1=cw[:, RR, :],
                                                   op0=ALU.mult, op1=ALU.add),
                    lambda: V.tensor_scalar(cw[:, R2, :], cw[:, RR, :], np.pi / 2, None, ALU.add),
                    lambda: V.tensor_scalar(cw[:, T2, :], cw[:, R2, :], np.pi, None, ALU.is_gt),
                    lambda: V.scalar_tensor_tensor(out=cw[:, R2, :], in0=cw[:, T2, :], scalar=-2 * np.pi, in1=cw[:, R2, :],
                                                   op0=ALU.mult, op1=ALU.add)]
                for s in steps:
                    dve_chain.tick(s())
                    dve_chain.settle(dve)
                for r in (RR, R2):
                    V.tensor_scalar(cw[:, r, :], cw[:, r, :], -PI_IN, PI_IN, ALU.max, ALU.min).then_inc(S("angle_ready"), 1)
                ln_stats(dve, X, "ln_in")
                for b, n in BLK:
                    ln_scale(X, X, b, n).then_inc(S("xn_ready"), 1)
                dve.wait_ge(S("mag_ready"), 1)
                dve.wait_ge(S("trig_ready"), 2)

                def op(dst, x, y, o):
                    dve_chain.tick(V.tensor_tensor(cw[:, dst, :], x if hasattr(x, "shape") else cw[:, x, :],
                                                   y if hasattr(y, "shape") else cw[:, y, :], o))

                lr, li = lam[:, 0, :], lam[:, 1, :]
                op(AR, MAG, COS, ALU.mult), op(AI, MAG, SIN, ALU.mult), op(T1, lr, lr, ALU.mult), op(T2, li, li, ALU.mult)
                dve_chain.settle(dve)
                op(DEN, T1, T2, ALU.add)
                dve_chain.tick(V.tensor_scalar(cw[:, A1, :], cw[:, AR, :], 1.0, None, ALU.subtract))
                dve_chain.settle(dve)
                dve_chain.tick(V.reciprocal(cw[:, DEN, :], cw[:, DEN, :]))
                op(T1, A1, lr, ALU.mult), op(T2, AI, li, ALU.mult)
                dve_chain.settle(dve)
                op(CR, T1, T2, ALU.add)
                op(T3, AI, lr, ALU.mult)
                dve_chain.settle(dve)
                op(T1, A1, li, ALU.mult)
                dve_chain.settle(dve)
                op(CI, T3, T1, ALU.subtract)
                dve_chain.settle(dve)
                op(CR, CR, DEN, ALU.mult), op(CI, CI, DEN, ALU.mult)
                dve_chain.settle(dve)
                V.tensor_copy(cw[:, T3, :], cw[:, T1, :]).then_inc(S("cw_ready"), 1)
                dve.wait_ge(S("co_ps"), 1)
                V.tensor_copy(co[:, :, :], bank[:, 6, 0:7 * NP].rearrange("p (i q) -> p i q", i=7))\
                 .then_inc(S("co_ready"), 1)
                dve.wait_ge(S("state_ps"), 1)
                dve_chain.tick(V.tensor_copy(H0, bank[:, 7, :].rearrange("p (c b q) -> p c b q", c=2, b=NB)))
                dve.wait_ge(S("vec_ps"), 1)
                V.tensor_copy(vT[:, :], bank[:, 6, 256:288]).then_inc(S("vec_ready"), 1)
                rotations(dve, 0, TBa)
                rotations(dve, 1, TBa)
                dve.wait_ge(S("adab_in"), 128)
                for v in range(2):
                    dve.wait_ge(used, KD * (v + 1))
                    V.tensor_tensor(mod01[:, v, :], bank[:, v, :], mod01[:, v, :], ALU.add).then_inc(S("mod_ready"), 1)
                dve.wait_ge(S("modt_ps"), 1)
                for g in range(4):
                    r = slice(32 * g, 32 * g + 32)
                    src = bank[r, 4 + g, 0:288].rearrange("p (v k r) -> p v k r", v=2, k=KD)
                    dve_chain.tick(V.tensor_copy(modT[r, 0, :, :], src[:, 0, :, :]))
                    dve_chain.tick(V.tensor_scalar(modT[r, 1, :, :], src[:, 1, :, :], 1.0, None, ALU.add))
                dve_chain.settle(dve)
                dve.wait_ge(S("xt_ready"), 12)
                smp = MT[:, :, SEQ:T].rearrange("p k (b t) -> p k b t", b=NB)
                dve_chain.tick(V.tensor_tensor(smp, smp, spread(modT[:, 1, :, 1:NROW], DS), ALU.mult))
                for k in range(KD):
                    V.tensor_scalar(MT[:, k, 0:SEQ], MT[:, k, 0:SEQ], modT[:, 1, k, 0:1], modT[:, 0, k, 0:1],
                                    ALU.mult, ALU.add).then_inc(S("ht_ready"), 1)
                dve_chain.settle(dve)
                V.tensor_tensor(smp, smp, spread(modT[:, 0, :, 1:NROW], DS), ALU.add).then_inc(S("ht_ready"), 1)

            @block.tensor
            def _(pe):
                pe.wait_ge(S("con_in"), 16)
                pe.wait_ge(S("silu_c"), 1)
                for k in range(KD):
                    mm = pe.transpose(bank[:, 7, NROW * k:NROW * k + NROW], crow[:, k:D:KD], ident[0:NROW, 0:NROW])
                mm.then_inc(S("ct_ps"), 1)
                pe.wait_ge(S("ct_ready"), 1)
                for k in range(KD):
                    ada_step(pe, 0, k, 0)
                for i in range(12):
                    b, n = BLK[i // 4]
                    pe.wait_ge(S("xn_ready"), b + 1)
                    if i >= 2:
                        pe.wait_ge(S("xt_ready"), i - 1)
                    for k in range(4):
                        kk = 4 * (i % 4) + k
                        mm = pe.transpose(bank[:, 2 + i % 2, n * k:n * k + n], X[0:n, b, kk:D:KD], ident[0:n, 0:n])
                    mm.then_inc(S("xt_ps"), 1)
                pe.wait_ge(S("cw_ready"), 1)
                for i in range(7):
                    mm = pe.transpose(bank[:, 6, NP * i:NP * i + NP], cw[:, i, :], ident[0:NP, 0:NP])
                mm.then_inc(S("co_ps"), 1)
                pe.wait_ge(S("vec_in"), 64)
                pe.wait_ge(S("co_ready"), 1)
                pe.transpose(bank[:, 6, 256:288], vrow, ident[0:32, 0:32]).then_inc(S("vec_ps"), 1)
                pe.wait_ge(S("state_in"), 32)
                for c in range(2):
                    for j in range(2):
                        mm = pe.transpose(bank[:, 7, 256 * c + P * j:256 * c + P * j + P], srow[:, j, c, :], ident)
                mm.then_inc(S("state_ps"), 1)
                for k in range(KD):
                    ada_step(pe, 1, k, 1)
                pe.wait_ge(S("c_in"), 16 * 16)
                pe.wait_ge(S("bw_ready"), 4)
                for i in range(8):
                    if i >= 2:
                        pe.wait_ge(S("bct_ready"), i - 1)
                    w = i // 2
                    for m in range(4):
                        mt = 4 * (i % 2) + m
                        src = Bw[:, w, 4 * mt:4 * mt + 4, :].rearrange("p q n -> p (q n)") if w < 2 else Cw[:, w - 2, mt, :]
                        mm = pe.transpose(bank[:, 4 + i % 2, P * m:P * m + P], src, ident)
                    mm.then_inc(S("bct_ps"), 1)
                pe.wait_ge(S("bct_ready"), 8)
                pe.wait_ge(S("mod_ready"), 2)
                pe.wait_ge(S("vec_ready"), 1)
                for v in range(2):
                    for k in range(KD):
                        for g in range(4):
                            r = slice(32 * g, 32 * g + NROW)
                            col = (v * KD + k) * NROW
                            mm = pe.matmul(bank[32 * g:32 * g + 32, 4 + g, col:col + NROW], mod01[r, v, k:512:KD],
                                           ident[r, 32 * g:32 * g + NROW], start=True, stop=True)
                mm.then_inc(S("modt_ps"), 1)

        TBb = Hf[:, 2048:3072].rearrange("p (i q t) -> p i q t", i=2, q=4)
        rot_in = Hf[:, 0:2048].rearrange("p (i q t) -> p i q t", i=4, q=2)
        g_buf = GEf[:, 0:2048].rearrange("p (b c q t) -> p b c q t", b=2, c=2, q=2)
        rot_out = ring[:, 8, :].rearrange("p (i q t) -> p i q t", i=4, q=2)
        h_buf = ring[:, 9, :].rearrange("p (b c q t) -> p b c q t", b=2, c=2, q=2)
        q_part = Xf[0:NS, 4608:6144].rearrange("p (j n) -> p j n", j=3)
        X_BANK, Y_BANK, ADA_BANK = (3, 4, 7), 5, 6
        NJ = NP // 2

        def rotation(j):
            q = 2 * (j % 2)
            return tab[:, (j // 2) % 2, 0, q:q + 2, :], tab[:, (j // 2) % 2, 1, q:q + 2, :]

        with nc.Block() as block:
            @block.sync
            def _(sp):
                load_chunks(sp, n_a + PRE_RING, n_b + PRE_RING)

            @block.scalar
            def _(act):
                act.wait_ge(used, n_a + 8)
                for m in range(0, 8, 2):
                    nc.scalar.copy(UT[:, m, :], bank[:, m, 0:T]).then_inc(S("u_ready"), 1)
                for c in range(3):
                    act.wait_ge(used, first[("qkv", c, 3)] + 1)
                    if c:
                        act.wait_ge(S("q_part_used"), c)
                    for i in range(6):
                        n, b = (P, i) if i < 2 else (NS, 2)
                        r = 32 * (i - 2) if i > 2 else 0
                        dst = q_part[:, i - 3, :] if i > 2 else qkv[0:n, b, 512 * c:512 * c + 512]
                        src = bank[r:r + n, b, :]
                        if c < 2:
                            dst = dst.rearrange("p (r g d) -> p g r d", r=REP, g=2)
                            src = src.rearrange("p (g r d) -> p g r d", r=REP, g=2)
                        nc.scalar.copy(dst, src).then_inc(S("qkv_free"), 1)

            @block.gpsimd
            def _(pool):
                for j in range(NJ):
                    pool.wait_ge(S("scan_ready"), 4 * j + 4)
                    c, s = rotation(j)
                    gr, gi = g_buf[:, j % 2, 0, :, :], g_buf[:, j % 2, 1, :, :]
                    for i, (x, y) in enumerate(((c, gr), (s, gi), (s, gr))):
                        pool_chain.tick(nc.gpsimd.tensor_tensor(rot_out[:, i, :, :], x, y, ALU.mult))
                    nc.gpsimd.tensor_tensor(rot_out[:, 3, :, :], c, gi, ALU.mult).then_inc(S("scan_free"), 1)
                    if j >= 2:
                        pool.wait_ge(S("y_pair"), j - 1)
                    pool.wait_ge(S("scan_free"), j + 1)
                    pool_chain.settle(pool)
                    nc.gpsimd.tensor_tensor(h_buf[:, j % 2, 0, :, :], rot_out[:, 0, :, :], rot_out[:, 1, :, :],
                                            ALU.subtract).then_inc(S("h_ready"), 1)
                    nc.gpsimd.tensor_tensor(h_buf[:, j % 2, 1, :, :], rot_out[:, 2, :, :], rot_out[:, 3, :, :],
                                            ALU.add).then_inc(S("h_ready"), 1)
                    pool.wait_ge(S("h_ready"), 2 * j + 2)
                    pool_chain.tick(nc.gpsimd.tensor_copy(HF[:, :, 2 * j:2 * j + 2], h_buf[:, j % 2, :, :, SEQ - 1]))
                pool_chain.settle(pool)

            @block.vector
            def _(dve):
                V = nc.vector

                def tt(dst, x, y, o):
                    dve_chain.tick(V.tensor_tensor(dst, x, y, o))

                dve.wait_ge(used, n_a + 8)
                for m in range(1, 8, 2):
                    V.tensor_copy(UT[:, m, :], bank[:, m, 0:T]).then_inc(S("u_ready"), 1)
                for q in range(4):
                    dve.wait_ge(S("xs_ps"), q + 1)
                    V.tensor_copy(XSf[:, q:NP:4, :, :], bank[:, q, :].rearrange("p (m c n) -> p m c n", m=8, c=2))\
                     .then_inc(S("xs_ready"), 1)
                dve.wait_ge(S("xs_ready"), 4)
                are, aim = spread(co[:, AR, :], NB), spread(co[:, AI, :], NB)
                w = [Wk[:, 8 + i, :].rearrange("p (q b) -> p q b", q=NP) for i in range(4)]

                def sample_step(t):
                    if t == 0:
                        hr, hi = (H0[:, c, :, :].rearrange("p b q -> p q b") for c in range(2))
                    else:
                        hr, hi = (XS[:, :, c, :, t - 1] for c in range(2))
                    tt(w[0], are, hr, ALU.mult), tt(w[1], aim, hi, ALU.mult)
                    tt(w[2], are, hi, ALU.mult), tt(w[3], aim, hr, ALU.mult)
                    dve_chain.settle(dve)
                    tt(w[0], w[0], w[1], ALU.subtract), tt(w[2], w[2], w[3], ALU.add)
                    dve_chain.settle(dve)
                    for c in range(2):
                        V.tensor_tensor(XS[:, :, c, :, t], XS[:, :, c, :, t], w[2 * c], ALU.add)\
                         .then_inc(S("xs_steps"), 1)
                    dve.wait_ge(S("xs_steps"), 2 * t + 2)

                def finish(m):
                    dve.wait_ge(S("y_pair"), 2 * m + 2)
                    V.scalar_tensor_tensor(out=UT[:, m, :], in0=UT[:, m, :], scalar=vT[:, 24 + m:25 + m],
                                           in1=bank[:, Y_BANK, 0:T], op0=ALU.mult, op1=ALU.add)\
                     .then_inc(S("y_free"), 1)

                def mod_out(v):
                    dve.wait_ge(used, first[("ada", v, KD - 1)] + 1)
                    V.tensor_tensor(MOD[:, v - 2, :], bank[:, ADA_BANK, :], MOD[:, v - 2, :], ALU.add)\
                     .then_inc(S("mod_ready"), 1)

                def add_parts(c):
                    dve.wait_ge(S("qkv_free"), 6 * c + 6)
                    dst = qkv[0:NS, 2, 512 * c:512 * c + 512]
                    for j in range(3):
                        if j < 2:
                            tt(dst, dst, q_part[:, j, :], ALU.add)
                            dve_chain.settle(dve)
                        else:
                            V.tensor_tensor(dst, dst, q_part[:, j, :], ALU.add).then_inc(S("q_part_used"), 1)

                for j in range(NJ):
                    if j % 2 == 0 and 1 <= j // 2 < 7:
                        dve.wait_ge(S("scan_free"), j)
                        rotations(dve, j // 2 + 1, TBb)
                    if j % 2 == 0 and j >= 4:
                        finish(j // 2 - 2)
                    c, s = rotation(j)
                    for q in range(2):
                        p = 2 * j + q
                        dve.wait_ge(S("ssmx_ps"), p + 1)
                        xr, xi = bank[:, X_BANK[p % 3], 0:SEQ], bank[:, X_BANK[p % 3], SEQ:2 * SEQ]
                        tt(rot_in[:, 0, q, :], c[:, q, :], xr, ALU.mult), tt(rot_in[:, 1, q, :], s[:, q, :], xi, ALU.mult)
                        tt(rot_in[:, 2, q, :], c[:, q, :], xi, ALU.mult)
                        V.tensor_tensor(rot_in[:, 3, q, :], s[:, q, :], xr, ALU.mult).then_inc(S("ssmx_free"), 1)
                    dve_chain.settle(dve)
                    tt(rot_in[:, 0, :, :], rot_in[:, 0, :, :], rot_in[:, 1, :, :], ALU.add)
                    dve.wait_ge(S("ssmx_free"), 2 * j + 2)
                    tt(rot_in[:, 2, :, :], rot_in[:, 2, :, :], rot_in[:, 3, :, :], ALU.subtract)
                    dve_chain.settle(dve)
                    if j >= 2:
                        dve.wait_ge(S("scan_free"), j - 1)
                    for q in range(2):
                        r = co[:, MAG, 2 * j + q:2 * j + q + 1].to_broadcast([P, SEQ])
                        for i in range(2):
                            V.tensor_tensor_scan(g_buf[:, j % 2, i, q, :], r, rot_in[:, 2 * i, q, :], 0.0,
                                                 ALU.mult, ALU.add).then_inc(S("scan_ready"), 1)
                    dve.wait_ge(S("scan_ready"), 4 * j + 4)
                    if j < 2:
                        sample_step(2 * j)
                        sample_step(2 * j + 1)
                    if ADA_STEPS * (j + 1) // KD > ADA_STEPS * j // KD:
                        mod_out(1 + ADA_STEPS * (j + 1) // KD)
                    if j in (4, 8, 12):
                        add_parts(j // 4 - 1)
                finish(6)
                finish(7)
                dve.wait_ge(S("q_part_used"), 3)
                dve.wait_ge(S("qkv_free"), 18)
                for b, n in BLK:
                    v = qkv[0:n, b, 0:1280].rearrange("p (h d) -> p h d", h=20)
                    x1, x2 = v[:, :, 0:8], v[:, :, 8:16]
                    cs = spread_mid(con[0:n, C_ROT + 16 * b:C_ROT + 16 * b + 8], 20)
                    sn = spread_mid(con[0:n, C_ROT + 16 * b + 8:C_ROT + 16 * b + 16], 20)
                    w = [Wk[0:n, i, 0:160].rearrange("p (h d) -> p h d", h=20) for i in range(4)]
                    tt(w[0], x1, cs, ALU.mult), tt(w[1], x2, sn, ALU.mult)
                    tt(w[2], x2, cs, ALU.mult), tt(w[3], x1, sn, ALU.mult)
                    dve_chain.settle(dve)
                    tt(x1, w[0], w[1], ALU.subtract), tt(x2, w[2], w[3], ALU.add)
                    dve_chain.settle(dve)

            @block.tensor
            def _(pe):
                for i in range(8):
                    w = arrived(pe, n_a + i).rearrange("p (k n) -> p k n", k=2)
                    for m in range(8):
                        for k in range(2):
                            mm = pe.matmul(bank[:, m, 0:T], w[:, k, P * m:P * m + P], MT[:, 2 * i + k, :],
                                           start=(i == 0 and k == 0), stop=(i == 7 and k == 1))
                    mm.then_inc(used, 1)
                pe.wait_ge(S("u_ready"), 8)
                for m in range(8):
                    for c in range(2):
                        for q in range(4):
                            r = slice(32 * q, 32 * q + 32)
                            mm = pe.matmul(bank[:, q, 64 * m + 32 * c:64 * m + 32 * c + 32], BT[c][r, m, :],
                                           UT[r, m, SEQ:T], start=True, stop=True)
                            if m == 7 and c == 1:
                                mm.then_inc(S("xs_ps"), 1)
                pe.wait_ge(S("xs_ready"), 4)

                def ssm_in(ps):
                    for p in ps:
                        if p >= 3:
                            pe.wait_ge(S("ssmx_free"), p - 2)
                    for c in range(2):
                        for p in ps:
                            m, r = p // 4, slice(32 * (p % 4), 32 * (p % 4) + 32)
                            mm = pe.matmul(bank[:, X_BANK[p % 3], SEQ * c:SEQ * c + SEQ], BT[c][r, m, :],
                                           UT[r, m, 0:SEQ], start=True, stop=True)
                            if c == 1:
                                mm.then_inc(S("ssmx_ps"), 1)

                def ssm_out(j):
                    m = j // 2
                    if j % 2 == 0 and m >= 1:
                        pe.wait_ge(S("y_free"), m)
                    pe.wait_ge(S("xs_steps"), 2 * DS)
                    pe.wait_ge(S("h_ready"), 2 * j + 2)
                    for smp in (True, False):
                        for c in range(2):
                            for q in range(2):
                                p = 2 * j + q
                                r = slice(32 * (p % 4), 32 * (p % 4) + 32)
                                cols, h = (slice(SEQ, T), XSf[:, p, c, :]) if smp else (slice(0, SEQ), h_buf[:, j % 2, c, q, :])
                                mm = pe.matmul(bank[r, Y_BANK, cols], CT[c][:, m, r], h, start=(c == 0), stop=(c == 1))
                    mm.then_inc(S("y_pair"), 1)

                ssm_in([0])
                ssm_in([1, 2])
                for j in range(NJ + 2):
                    if j < NJ:
                        for s in range(ADA_STEPS * j, ADA_STEPS * (j + 1)):
                            v, k = 2 + s // KD, s % KD
                            if k == 0:
                                pe.wait_ge(S("mod_ready"), v)
                            ada_step(pe, v, k, ADA_BANK)
                        if j < 12:
                            c, i = j // 4, j % 4
                            if i == 0 and c > 0:
                                pe.wait_ge(S("qkv_free"), 6 * c)
                            w = arrived(pe, first[("qkv", c, i)]).rearrange("p (k n) -> p k n", k=4)
                            for k in range(4):
                                for b in range(2):
                                    pe.matmul(bank[:, b, :], MT[:, 4 * i + k, P * b:P * b + P], w[:, k, :],
                                              start=(i == 0 and k == 0), stop=(i == 3 and k == 3))
                            for k in range(4):
                                mm = pe.matmul(bank[32 * k:32 * k + 32, 2, :], MT[:, 4 * i + k, SEQ:T], w[:, k, :],
                                               start=(i == 0), stop=(i == 3))
                            mm.then_inc(used, 1)
                        ssm_in([p for p in (2 * j + 3, 2 * j + 4) if p < NP])
                    if j >= 2:
                        ssm_out(j - 2)

        HS = Wk[:, 0:2, :].rearrange("p c (b q) -> p c b q", b=NB)
        SR = Wk[:, 2:4, :].rearrange("p c (j n) -> p c j n", j=2)
        FR = Wk[0:64, 4, 0:P]
        GSQ = GEf[:, 2944:3968]
        Ps = Hf[:, 0:1280].rearrange("p (b w) -> p b w", b=NB)
        PTc = Hf[:, 1280:2304].rearrange("p (b r) -> p b r", b=NB)
        PTn = Hf[0:NS, 2304:3328].rearrange("p (b r) -> p b r", b=NB)
        OS = Xf[:, 4608:5120].rearrange("p (b d) -> p b d", b=NB)
        att = qkv[:, :, 0:DA]
        UNITS = [(n, g) for n in range(2) for g in range(NKV)]

        with nc.Block() as block:
            @block.sync
            def _(sp):
                load_chunks(sp, n_b + PRE_RING, n_c + PRE_RING)
                sp.wait_ge(S("hs_rows"), 5)
                for c, s in ((0, "re"), (1, "im")):
                    sp.dma_start(o["ssm_%s_prompt" % s].rearrange("o b (q h) n -> (o b q) (h n)", h=2), FR[32 * c:32 * c + 32, :])\
                      .then_inc(S("state_out"), 16)
                    sp.dma_start(o["ssm_%s_sample" % s][0].rearrange("(j b) (q h) n -> (b q) j (h n)", j=2, h=2), SR[:, c, :, :])\
                      .then_inc(S("state_out"), 16)
                sp.wait_ge(S("state_out"), 64)
                sp.nop().then_inc(S("wk_free"), 1)
                sp.wait_ge(S("so_ready"), 1)
                for g in range(NKV):
                    for r in range(REP):
                        sp.dma_start(attn_dram.rearrange("(b t) (h d) -> h t b d", b=NB, h=NH)[REP * g + r],
                                     OS[32 * g + 4 * r:32 * g + 4 * r + 4, :, :]).then_inc(S("so_out"), 16)
                sp.wait_ge(S("so_out"), 256)
                sp.dma_start(att[0:NS, 2, :], attn_dram).then_inc(S("so_in"), 16)
                sp.wait_ge(S("kv_out"), 16 * 20)

            @block.gpsimd
            def _(pool):
                pool.dma_start(mask, a["masks"]).then_inc(S("mask_in"), 16)
                pool.dma_start(sink[:, :], a["attn_sinks"].to_broadcast([P, NH])).then_inc(S("sink_in"), 16)
                pool_chain.tick(nc.gpsimd.memset(sinkc[:, :], 0.0))
                pool_chain.tick(nc.gpsimd.memset(QS[:, :, :, :], 0.0))
                pool_chain.settle(pool)
                for g in range(NKV):
                    pool.dma_start(sinkc[32 * g:32 * g + 16, :],
                                   a["attn_sinks"][0, 4 * g:4 * g + 4].unsqueeze(1).to_broadcast([4, 4]).unsqueeze(2))\
                        .then_inc(S("sink_in"), 16)
                pool.wait_ge(S("kc_in"), 16)
                pool.wait_ge(S("vc_in"), 16)
                for i, s in ((0, "k"), (1, "v")):
                    cache = (KC, VC)[i]
                    new = slice(DA + DKV * i, DA + DKV * i + DKV)
                    pool.dma_start(o[s + "_win_prompt"].rearrange("o b w g d -> (o b w) (g d)"), qkv[:, 1, new])\
                        .then_inc(S("kv_out"), 16)
                    dst = o[s + "_win_sample"][0].rearrange("b w g d -> w b (g d)")
                    pool.dma_start(dst[0:WIN - DS], cache[DS:WIN, :, :]).then_inc(S("kv_out"), 16)
                    for b in range(NB):
                        pool.dma_start(dst[WIN - DS:WIN, b, :], qkv[DS * b:DS * b + DS, 2, new]).then_inc(S("kv_out"), 16)
                pool.wait_ge(S("qt_ready"), 9)
                for g in range(2):
                    for r in range(REP):
                        nc.gpsimd.tensor_copy(QS[:, :, g, 4 * r:4 * r + 4],
                                              QT[:, 4 * g + r, SEQ:T].rearrange("p (b t) -> p b t", b=NB))\
                            .then_inc(S("qs_ready"), 1)
                pool.wait_ge(S("qs_ready"), 8)

            @block.scalar
            def _(act):
                act.dma_start(KC, a["cache_k_win"][0].rearrange("b w g d -> w b (g d)")).then_inc(S("kc_in"), 16)
                act.dma_start(VC, a["cache_v_win"][0].rearrange("b w g d -> w b (g d)")).then_inc(S("vc_in"), 16)
                for i in range(9):
                    b, n = BLK[i // 3]
                    act.wait_ge(S("qt_ps"), i + 1)
                    j = i % 3
                    dst = QT[:, 4 * j:4 * j + 4, P * b:P * b + n] if j < 2 else KT[:, :, P * b:P * b + n]
                    w = dst.shape[1]
                    nc.scalar.copy(dst, bank[:, i % 2, 0:w * n].rearrange("p (i t) -> p i t", i=w))\
                      .then_inc(S("qt_ready"), 1)
                for i in range(4):
                    act.wait_ge(S("kct_ps"), i + 1)
                    nc.scalar.copy(kcT[:, 2 * i:2 * i + 2, :, :],
                                   bank[:, 2 + i % 2, :].rearrange("p (b g w) -> p b g w", b=2, g=2))\
                      .then_inc(S("kct_ready"), 1)
                for i in range(5):
                    act.wait_ge(S("hs_ps"), i + 1)
                    dst = FR if i == 0 else SR[:, (i - 1) // 2, (i - 1) % 2, :]
                    nc.scalar.copy(dst, bank[0:dst.shape[0], 4 + i % 2, 0:P]).then_inc(S("hs_rows"), 1)
                for i, (n, g) in enumerate(UNITS):
                    w = slice(0, 2 * P) if n else slice(P, 2 * P)
                    act.wait_ge(S("negmax_ready"), i + 1)
                    for r in range(REP):
                        nc.scalar.activation(Pb[:, r, w], Pb[:, r, w], ACT.Exp, bias=nm[:, r:r + 1],
                                             accum_out=den[:, r:r + 1]).then_inc(S("p_ready"), 1)
                    nc.scalar.activation(esink[:, 0:4], smx[:, 0:4], ACT.Exp).then_inc(S("esink_ready"), 1)
                    act.wait_ge(S("pt_ps"), i + 1)
                    if i >= 1:
                        act.wait_ge(S("o_ps"), i)
                    for j in ((0, 1) if n else (1,)):
                        nc.scalar.copy(PT[:, j, :, :], bank[:, 4 + j, :].rearrange("p (h q) -> p h q", h=4))\
                          .then_inc(S("pt_ready"), 1)
                act.wait_ge(S("snegmax_ready"), 1)
                for b in range(NB):
                    nc.scalar.activation(Ps[:, b, :], Ps[:, b, :], ACT.Exp, bias=snm[:, b:b + 1],
                                         accum_out=sden[:, b:b + 1]).then_inc(S("sp_ready"), 1)
                nc.scalar.activation(sesink[:, :], ssmx[:, :], ACT.Exp).then_inc(S("sesink_ready"), 1)
                for i in range(4):
                    act.wait_ge(S("spt_ps"), i + 1)
                    dst = (PTc if i < 2 else PTn)[:, 4 * (i % 2):4 * (i % 2) + 4, :]
                    nc.scalar.copy(dst, bank[0:dst.shape[0], i, :].rearrange("p (b r) -> p b r", b=4))\
                      .then_inc(S("spt_ready"), 1)
                act.wait_ge(S("spt_ready"), 4)
                for b, n in BLK:
                    if b == 2:
                        act.wait_ge(S("so_in"), 16)
                    else:
                        act.wait_ge(S("o_ready"), 8)
                    nc.scalar.activation(GSQ[0:n, :], att[0:n, b, :], ACT.Square, accum_out=ssq[0:n, b:b + 1])\
                      .then_inc(S("ssq_ready"), 1)
                    act.wait_ge(S("msq_ready"), b + 1)
                    nc.scalar.activation(rms[0:n, b:b + 1], ssq[0:n, b:b + 1], ACT.Sqrt).then_inc(S("rms_ready"), 1)
                    for i in (2 * b, 2 * b + 1):
                        act.wait_ge(S("mt_ps"), i + 1)
                        for k in range(4):
                            f = 4 * (i % 2) + k
                            last = nc.scalar.mul(MT[:, f, P * b:P * b + n], bank[:, i % 2, n * k:n * k + n], vT[:, f:f + 1])
                        last.then_inc(S("mt_free"), 1)

            @block.vector
            def _(dve):
                V = nc.vector

                def tt(dst, x, y, o):
                    dve_chain.tick(V.tensor_tensor(dst, x, y, o))

                V.tensor_copy(HS, XS[:, :, :, :, DS - 1].rearrange("p q c b -> p c b q")).then_inc(S("hs_ready"), 1)
                dve.wait_ge(S("mask_in"), 16)
                dve.wait_ge(S("sink_in"), 16 * 5)

                def mod_out(v):
                    dve.wait_ge(used, first[("ada", v, KD - 1)] + 1)
                    V.tensor_tensor(MOD[:, v - 2, :], bank[:, 7, :], MOD[:, v - 2, :], ALU.add).then_inc(S("mod_ready"), 1)

                for i, (n, g) in enumerate(UNITS):
                    w = slice(0, 2 * P) if n else slice(P, 2 * P)
                    if i:
                        dve.wait_ge(S("pt_ps"), i)
                    dve.wait_ge(S("s_ps"), i + 1)
                    if n:
                        for h in range(2):
                            src = bank[:, 2 * (i % 2) + h, :].rearrange("p (h w) -> p h w", h=2)
                            dve_chain.tick(V.scalar_tensor_tensor(
                                out=Pb[:, 2 * h:2 * h + 2, :], in0=src, scalar=HD ** -0.5,
                                in1=spread_mid(mask[:, M_PREV:M_PREV + 2 * P], 2), op0=ALU.mult, op1=ALU.add))
                    else:
                        dve_chain.tick(V.scalar_tensor_tensor(
                            out=Pb[:, :, w], in0=bank[:, 2 * (i % 2), :].rearrange("p (h w) -> p h w", h=4),
                            scalar=HD ** -0.5, in1=spread_mid(mask[:, M_SELF:M_SELF + P], 4), op0=ALU.mult, op1=ALU.add))
                    dve_chain.settle(dve)
                    dve_chain.tick(V.tensor_reduce(mx[:, :], Pb[:, :, w], AX.X, ALU.max))
                    dve_chain.settle(dve)
                    sk = sink[:, 4 * g:4 * g + 4]
                    tt(mx[:, :], mx[:, :], sk, ALU.max)
                    dve_chain.settle(dve)
                    tt(smx[:, :], sk, mx[:, :], ALU.subtract)
                    dve_chain.settle(dve)
                    V.tensor_scalar(nm[:, :], mx[:, :], -1.0, None, ALU.mult).then_inc(S("negmax_ready"), 1)
                    dve.wait_ge(S("p_ready"), 4 * i + 4)
                    dve.wait_ge(S("esink_ready"), i + 1)
                    tt(rd[:, :], den[:, :], esink[:, :], ALU.add)
                    dve_chain.settle(dve)
                    dve_chain.tick(V.reciprocal(rd[:, :], rd[:, :]))
                    dve_chain.settle(dve)
                    dve.wait_ge(S("o_ps"), i + 1)
                    V.tensor_tensor(att[:, n, 256 * g:256 * g + 256].rearrange("p (h d) -> p h d", h=4),
                                    bank[:, 6, 0:256].rearrange("p (h d) -> p h d", h=4), spread(rd[:, :], HD), ALU.mult)\
                     .then_inc(S("o_ready"), 1)
                    if i == len(UNITS) - 1:
                        mod_out(5)
                dve.wait_ge(S("wk_free"), 1)
                dve.wait_ge(S("ss_ps"), 1)
                for g in range(NKV):
                    r = slice(32 * g, 32 * g + 32)
                    for j in range(3):
                        nb = min(3, NB - 3 * j)
                        src = bank[r, 3 * (g % 2) + j, 0:160 * nb].rearrange("p (b w) -> p b w", b=nb)
                        bs = slice(3 * j, 3 * j + nb)
                        dve_chain.tick(V.scalar_tensor_tensor(
                            out=Ps[r, bs, 0:WIN], in0=src[:, :, 0:WIN], scalar=HD ** -0.5,
                            in1=spread_mid(mask[r, M_CACHE:M_CACHE + WIN], nb), op0=ALU.mult, op1=ALU.add))
                        dve_chain.tick(V.scalar_tensor_tensor(
                            out=Ps[r, bs, WIN:160], in0=src[:, :, WIN:160], scalar=HD ** -0.5,
                            in1=mask[r, M_NEW + 96 * j:M_NEW + 96 * j + 32 * nb].rearrange("p (b w) -> p b w", b=nb),
                            op0=ALU.mult, op1=ALU.add))
                dve_chain.settle(dve)
                dve_chain.tick(V.tensor_reduce(smxx[:, :], Ps, AX.X, ALU.max))
                dve_chain.settle(dve)
                dve_chain.tick(V.tensor_scalar(smxx[:, :], smxx[:, :], sinkc[:, 0:1], None, ALU.max))
                dve_chain.settle(dve)
                dve_chain.tick(V.tensor_scalar(ssmx[:, :], smxx[:, :], -1.0, sinkc[:, 0:1], ALU.mult, ALU.add))
                dve_chain.settle(dve)
                V.tensor_scalar(snm[:, :], smxx[:, :], -1.0, None, ALU.mult).then_inc(S("snegmax_ready"), 1)
                dve.wait_ge(S("sp_ready"), 8)
                dve.wait_ge(S("sesink_ready"), 1)
                tt(sden[:, :], sden[:, :], sesink[:, :], ALU.add)
                dve_chain.settle(dve)
                dve_chain.tick(V.reciprocal(sden[:, :], sden[:, :]))
                dve_chain.settle(dve)
                dve.wait_ge(S("so_ps"), 1)
                V.tensor_tensor(OS, bank[:, 5, :].rearrange("p (b d) -> p b d", b=NB), spread(sden[:, :], HD), ALU.mult)\
                 .then_inc(S("so_ready"), 1)
                for b, n in BLK:
                    dve.wait_ge(S("ssq_ready"), b + 1)
                    V.tensor_scalar(ssq[0:n, b:b + 1], ssq[0:n, b:b + 1], 1.0 / DA, EPS, ALU.mult, ALU.add)\
                     .then_inc(S("msq_ready"), 1)
                    dve.wait_ge(S("rms_ready"), b + 1)
                    dve_chain.tick(V.reciprocal(rms[0:n, b:b + 1], rms[0:n, b:b + 1]))
                    dve_chain.settle(dve)
                    V.tensor_scalar(att[0:n, b, :], att[0:n, b, :], rms[0:n, b:b + 1], None, ALU.mult)\
                     .then_inc(S("attn_ready"), 1)

            @block.tensor
            def _(pe):
                for i in range(9):
                    b, n = BLK[i // 3]
                    j = i % 3
                    if i >= 2:
                        pe.wait_ge(S("qt_ready"), i - 1)
                    for x in range(4 if j < 2 else 2):
                        f = 512 * j + P * x
                        mm = pe.transpose(bank[:, i % 2, n * x:n * x + n], qkv[0:n, b, f:f + P], ident[0:n, 0:n])
                    mm.then_inc(S("qt_ps"), 1)
                pe.wait_ge(S("kc_in"), 16)
                for i in range(4):
                    if i >= 2:
                        pe.wait_ge(S("kct_ready"), i - 1)
                    for x in range(4):
                        mm = pe.transpose(bank[:, 2 + i % 2, P * x:P * x + P],
                                          KC[:, 2 * i + x // 2, P * (x % 2):P * (x % 2) + P], ident)
                    mm.then_inc(S("kct_ps"), 1)
                pe.wait_ge(S("hs_ready"), 1)
                for i in range(5):
                    if i >= 2:
                        pe.wait_ge(S("hs_rows"), i - 1)
                    if i == 0:
                        mm = pe.transpose(bank[0:64, 4, 0:P], HF[:, :, :].rearrange("p c q -> p (c q)"), ident)
                    else:
                        c, j = (i - 1) // 2, (i - 1) % 2
                        mm = pe.transpose(bank[:, 4 + i % 2, 0:P],
                                          HS[:, c, 4 * j:4 * j + 4, :].rearrange("p b q -> p (b q)"), ident)
                    mm.then_inc(S("hs_ps"), 1)
                pe.wait_ge(S("qt_ready"), 9)
                pe.wait_ge(S("kct_ready"), 4)
                pe.wait_ge(S("hs_rows"), 5)

                def scores(i):
                    n, g = UNITS[i]
                    h = slice(64 * (g % 2), 64 * (g % 2) + 64)
                    w = 2 * P if n else P
                    if i >= 2:
                        pe.wait_ge(S("negmax_ready"), i - 1)
                    for r in range(REP):
                        b = 2 * (i % 2) + (w * r) // 512
                        mm = pe.matmul(bank[:, b, (w * r) % 512:(w * r) % 512 + w],
                                       QT[h, 4 * (g // 2) + r, P * n:P * n + P], KT[h, g // 2, 0:w], start=True, stop=True)
                    mm.then_inc(S("s_ps"), 1)

                scores(0)
                for i, (n, g) in enumerate(UNITS):
                    if i + 1 < len(UNITS):
                        scores(i + 1)
                    for k in range(2 * i, 2 * i + 2):
                        ada_step(pe, 5, k, 7)
                    pe.wait_ge(S("p_ready"), 4 * i + 4)
                    if i:
                        pe.wait_ge(S("pt_ready"), pt_count(i))
                    for j in ((0, 1) if n else (1,)):
                        for r in range(REP):
                            mm = pe.transpose(bank[:, 4 + j, P * r:P * r + P], Pb[:, r, P * j:P * j + P], ident)
                    mm.then_inc(S("pt_ps"), 1)
                    pe.wait_ge(S("pt_ready"), pt_count(i + 1))
                    if i:
                        pe.wait_ge(S("o_ready"), i)
                    js = (0, 1) if n else (1,)
                    for r in range(REP):
                        for j in js:
                            mm = pe.matmul(bank[:, 6, HD * r:HD * r + HD], PT[:, j, r, :],
                                           qkv[:, n - 1 + j, DA + DKV + HD * g:DA + DKV + HD * g + HD],
                                           start=(j == js[0]), stop=(j == 1))
                    mm.then_inc(S("o_ps"), 1)
                pe.wait_ge(S("qs_ready"), 8)
                for b in range(NB):
                    for g in range(NKV):
                        h = slice(64 * (g % 2), 64 * (g % 2) + 64)
                        out = bank[32 * g:32 * g + 32, 3 * (g % 2) + b // 3, 160 * (b % 3):160 * (b % 3) + 160]
                        pe.matmul(out[:, 0:WIN], QS[h, b, g // 2, :], kcT[h, b, g // 2, :], start=True, stop=True)
                        mm = pe.matmul(out[:, WIN:160], QS[h, b, g // 2, :], KT[h, g // 2, SEQ:T], start=True, stop=True)
                mm.then_inc(S("ss_ps"), 1)
                pe.wait_ge(S("sp_ready"), 8)
                for i in range(4):
                    w = slice(0, WIN) if i < 2 else slice(WIN, 160)
                    for b in range(4):
                        src = Ps[:, 4 * (i % 2) + b, w]
                        mm = pe.transpose(bank[0:src.shape[1], i, P * b:P * b + P], src, ident)
                    mm.then_inc(S("spt_ps"), 1)
                pe.wait_ge(S("vc_in"), 16)
                pe.wait_ge(S("spt_ready"), 4)
                for b in range(NB):
                    for g in range(NKV):
                        r = slice(32 * g, 32 * g + 32)
                        pe.matmul(bank[r, 5, HD * b:HD * b + HD], PTc[:, b, r], VC[:, b, HD * g:HD * g + HD],
                                  start=True, stop=False)
                        mm = pe.matmul(bank[r, 5, HD * b:HD * b + HD], PTn[:, b, r],
                                       qkv[0:NS, 2, DA + DKV + HD * g:DA + DKV + HD * g + HD], start=False, stop=True)
                mm.then_inc(S("so_ps"), 1)
                for i in range(6):
                    b, n = BLK[i // 2]
                    pe.wait_ge(S("attn_ready"), b + 1)
                    if i >= 2:
                        pe.wait_ge(S("mt_free"), i - 1)
                    for k in range(4):
                        f = P * (4 * (i % 2) + k)
                        mm = pe.transpose(bank[:, i % 2, n * k:n * k + n], att[0:n, b, f:f + P], ident[0:n, 0:n])
                    mm.then_inc(S("mt_ps"), 1)

        L = later
        tmpO = L[:, 0:2048]
        smpO = L[0:NS, 2048:4096]
        smpE = L[0:NS, 11136:12160]
        shS = L[0:NS, 4096:6144]
        sq = L[:, 4096:4096 + 8 * T].rearrange("p (m t) -> p m t", m=8)
        rs = L[:, 6400:6400 + T]
        rw = L[:, 6688:6688 + 576].rearrange("p (k e) -> p k e", k=KD)
        rwg = L[:, 7264:7328].rearrange("p (k e) -> p k e", k=KD)
        rwe = L[:, 7328:7840].rearrange("p (k e) -> p k e", k=KD)
        rbias = L[:, 7840:7876]
        rc = L[:, 9728:9728 + R_N]
        LG = L[:, 8064:8064 + 108].rearrange("p (b e) -> p b e", b=3)
        RT = L[:, 8192:8192 + 96 * 16].rearrange("p (i b e) -> p i b e", i=16, b=3)
        RQ = L[:, 6400:6400 + NBLK * E].rearrange("p (j e) -> p j e", j=NBLK)
        xf = L[:, 10240:10240 + NBLK]
        RK = L[:, 10752:10752 + 128].rearrange("p (b e) -> p b e", b=4)
        rsm = L[:, 10880:10880 + 96].rearrange("p (i b c) -> p i b c", i=8, b=3)
        zeros = L[:, 10240:12288]
        xt = L[:, 11008:11008 + 128].rearrange("p (i e) -> p i e", i=4)
        G2_BANKS = [4, 5, 6, 7, 0, 1, 4, 5]
        OUT_BANKS = [[(0, 1), (2, 3), 4], [(5, 6), (7, 0), 1]]
        EXPAND = [(v, n0, n, dst, g) for v, n0, n, dst in ((2, 0, P, H[:, 0, :]), (1, 0, P, H[:, 1, :]),
                                                           (2, P, NS, H[0:NS, 2, :]), (1, P, NS, shS)) for g in range(4)]

        G2 = MT[:, :, :].rearrange("p k t -> p (k t)")[:, 0:2 * D].rearrange("p (i d) -> p i d", i=2)
        with nc.Block() as block:
            @block.sync
            def _(sp):
                sp.dma_start(X[:, 0:2, :], a["x_prompt"][0].rearrange("(b p) d -> p b d", b=2)).then_inc(S("x_in"), 16)
                sp.dma_start(X[0:NS, 2, :], a["x_sample"].rearrange("b t d -> (b t) d")).then_inc(S("x_in"), 16)
                load_chunks(sp, n_c + PRE_RING, len(plan))
                sp.wait_ge(used, len(plan))
                for j in range(PRE_RING):
                    load_expert_chunk(sp, 0, j)
                sp.wait_ge(S("h2_ready"), 3)
                for j in range(PRE_RING, PRE_RING + 3):
                    load_expert_chunk(sp, 0, j)

            @block.gpsimd
            def _(pool):
                pool_chain.tick(nc.gpsimd.memset(zeros, 0.0))
                pool_chain.settle(pool)
                for r in range(E * SLOTS, NBLK * SLOTS, P):
                    n = min(P, NBLK * SLOTS - r)
                    pool.dma_start(y_dram[r:r + n, :], zeros[0:n, :]).then_inc(S("spare_out"), 16)
                pool.dma_start(BCf[:, 0:D], a["ln1_g"].to_broadcast([P, D])).then_inc(S("ln1_in"), 16)
                pool.dma_start(BCf[:, D:2 * D], a["ln1_b"].to_broadcast([P, D])).then_inc(S("ln1_in"), 16)
                pool.dma_start(rwg, a["router_group_w"][0].rearrange("(p k) e -> p k e", k=KD)).then_inc(S("rw_in"), 16)
                pool.dma_start(rwe, a["router_expert_w"][0].rearrange("(p k) e -> p k e", k=KD)).then_inc(S("rw_in"), 16)
                pool.dma_start(rbias[:, 0:NEG], a["router_group_b"].to_broadcast([P, NEG])).then_inc(S("rw_in"), 16)
                pool.dma_start(rbias[:, NEG:], a["router_expert_b"].to_broadcast([P, E])).then_inc(S("rw_in"), 16)
                pool.dma_start(rc, a["route_consts"]).then_inc(S("rw_in"), 16)
                pool.wait_ge(S("rw_in"), 80)
                nc.gpsimd.tensor_copy(rw[:, :, 0:NEG], rwg).then_inc(S("rw_ready"), 1)
                nc.gpsimd.tensor_copy(rw[:, :, NEG:], rwe).then_inc(S("rw_ready"), 1)
                for m in range(8):
                    pool.wait_ge(S("ssm_ready"), m + 1)
                    nc.gpsimd.tensor_tensor(sq[:, m, :], MT[:, 8 + m, :], MT[:, 8 + m, :], ALU.mult)\
                      .then_inc(S("sq_ready"), 1)
                pool.wait_ge(S("gx_ready"), 8)
                for h in range(2):
                    c = slice(1024 * h, 1024 * h + 1024)
                    pool.wait_ge(S("smp_ready"), 4 * h + 4)
                    nc.gpsimd.tensor_tensor(smpO[:, c], smpO[:, c], smpE, ALU.add).then_inc(S("smp_sum"), 1)
                    pool.wait_ge(S("smp_sum"), h + 1)
                    nc.gpsimd.tensor_tensor(smpO[:, c], smpO[:, c], GE[0:NS, 1, c], ALU.mult).then_inc(S("smp_gated"), 1)
                pool.wait_ge(S("smp_gated"), 2)
                pool.wait_ge(S("out_free"), 8)
                pool.dma_start(GE[:, 0, :], a["ln2_g"].to_broadcast([P, D])).then_inc(S("ln2_in"), 16)
                pool.dma_start(GE[:, 1, :], a["ln2_b"].to_broadcast([P, D])).then_inc(S("ln2_in"), 16)

            @block.scalar
            def _(act):
                nc.scalar.activation(UT[:, :, :], UT[:, :, :], ACT.Gelu_apprx_tanh).then_inc(S("z_ready"), 1)
                act.wait_ge(used, first[("glu", 3, 0)] + 1)
                for m in range(8):
                    nc.scalar.activation(MT[:, 8 + m, :], bank[:, m, 0:T], ACT.Sigmoid, bias=vT[:, 16 + m:17 + m])\
                      .then_inc(S("glu_sig"), 1)
                for i in range(8):
                    act.wait_ge(S("gx_ps"), i + 1)
                    n = P if i < 4 else NS
                    nc.scalar.copy(GE[0:n, i // 4, 512 * (i % 4):512 * (i % 4) + 512], bank[0:n, 6 + i % 2, :])\
                      .then_inc(S("gx_ready"), 1)
                act.wait_ge(S("rs_ms"), 1)
                nc.scalar.activation(rs, rs, ACT.Sqrt).then_inc(S("rs_sqrt"), 1)
                for h in range(2):
                    act.wait_ge(used, first[("out", h, 7)] + 1)
                    if h:
                        act.wait_ge(S("smp_sum"), 1)
                    else:
                        act.wait_ge(S("spare_out"), 16 * -(-XB * SLOTS // P))
                    for i in range(4):
                        k, c = i // 2, i % 2
                        dst = smpE[:, 512 * c:512 * c + 512] if k else smpO[:, 1024 * h + 512 * c:1024 * h + 512 * c + 512]
                        nc.scalar.copy(dst, bank[32 * i:32 * i + 32, OUT_BANKS[h][2], :]).then_inc(S("smp_ready"), 1)
                    if h == 0:
                        act.wait_ge(S("h_free"), 1)
                        for i, (v, n0, n, dst, g) in enumerate(EXPAND):
                            act.wait_ge(S("ex_ps"), i + 1)
                            nc.scalar.copy(dst[:, 512 * g:512 * g + 512], bank[0:n, 2 + i % 3, :])\
                              .then_inc(S("ex_ready"), 1)
                ln_sqrt(act, "ln1")
                for b in range(2):
                    ln_sqrt_of(act, "ln0", b, P)
                for i in range(12):
                    b, n = BLK[i // 4]
                    if i == 8:
                        ln_sqrt_of(act, "ln0", 2, NS)
                    act.wait_ge(S("h2t_ps"), i + 1)
                    nc.scalar.copy(MT[:, 4 * (i % 4):4 * (i % 4) + 4, P * b:P * b + n],
                                   bank[:, i % 2, 0:4 * n].rearrange("p (k t) -> p k t", k=4)).then_inc(S("h2t_ready"), 1)
                act.wait_ge(S("lg_sub"), 1)
                nc.scalar.activation(rsm[:, 1, :, :], rsm[:, 1, :, :], ACT.Exp).then_inc(S("lg_exp"), 1)
                act.wait_ge(S("lg_sub"), 2)
                nc.scalar.activation(rsm[:, 3, :, 0:1], rsm[:, 3, :, 0:1], ACT.Exp).then_inc(S("lg_exp"), 1)
                for i in range(8):
                    act.wait_ge(S("g2_ps"), i + 1)
                    n = P if i < 4 else NS
                    nc.scalar.copy(G2[0:n, i // 4, 512 * (i % 4):512 * (i % 4) + 512], bank[0:n, G2_BANKS[i], :])\
                      .then_inc(S("g2_ready"), 1)

            @block.vector
            def _(dve):
                V = nc.vector

                def go(*ins):
                    for i in ins:
                        dve_chain.tick(i)
                    dve_chain.settle(dve)

                dve_chain.tick(V.memset(LG, 0.0))
                V.tensor_scalar(MOD[:, 2, :], MOD[:, 2, :], 1.0, None, ALU.add).then_inc(S("scale2_one"), 1)
                for m in range(8):
                    dve.wait_ge(S("glu_sig"), m + 1)
                    V.tensor_tensor(MT[:, 8 + m, :], MT[:, 8 + m, :], UT[:, m, :], ALU.mult).then_inc(S("ssm_ready"), 1)
                dve.wait_ge(S("rs_ps"), 1)
                V.tensor_scalar(rs, bank[:, 5, 0:T], 1.0 / DSSM, EPS, ALU.mult, ALU.add).then_inc(S("rs_ms"), 1)
                dve.wait_ge(S("rs_sqrt"), 1)
                go(V.reciprocal(rs, rs))
                dve.wait_ge(S("sq_ready"), 8)
                for m in range(8):
                    V.scalar_tensor_tensor(out=MT[:, 8 + m, :], in0=MT[:, 8 + m, :], scalar=vT[:, 8 + m:9 + m], in1=rs,
                                           op0=ALU.mult, op1=ALU.mult).then_inc(S("ssmn_ready"), 1)
                for r in (slice(32, 64), slice(64, P)):
                    dve_chain.tick(V.memset(H[r, 2, :], 0.0))
                V.memset(RT[:, 0, 0, 0:1], 0.0).then_inc(S("h_free"), 1)
                dve.wait_ge(S("x_in"), 64)
                dve.wait_ge(S("gx_ready"), 8)
                for h in range(2):
                    cols = slice(1024 * h, 1024 * h + 1024)

                    def stats(b, n):
                        for c in (2 * h, 2 * h + 1):
                            dve_chain.tick(V.bn_stats(st[0:n, b, 6 * c:6 * c + 6], X[0:n, b, 512 * c:512 * c + 512]))

                    dve.wait_ge(used, first[("out", h, 7)] + 1)
                    for b in range(2):
                        for c in range(2):
                            V.tensor_tensor(tmpO[:, 1024 * b + 512 * c:1024 * b + 512 * c + 512], bank[:, OUT_BANKS[h][b][c], :],
                                            GE[:, 0, 1024 * h + 512 * c:1024 * h + 512 * c + 512], ALU.mult)\
                             .then_inc(S("out_free"), 1)
                        dve.wait_ge(S("out_free"), 4 * h + 2 * b + 2)
                        go(V.scalar_tensor_tensor(out=X[:, b, cols], in0=X[:, b, cols], scalar=ALPHA,
                                                  in1=tmpO[:, 1024 * b:1024 * b + 1024], op0=ALU.mult, op1=ALU.add))
                        stats(b, P)
                    dve.wait_ge(S("smp_gated"), h + 1)
                    go(V.scalar_tensor_tensor(out=X[0:NS, 2, cols], in0=X[0:NS, 2, cols], scalar=ALPHA, in1=smpO[:, cols],
                                              op0=ALU.mult, op1=ALU.add))
                    stats(2, NS)
                dve_chain.settle(dve)
                ln_finish(dve, "ln1")
                dve.wait_ge(S("ln1_in"), 32)

                def ln1(b, n):
                    x, s = X[0:n, b, :], st[0:n, b, :]
                    go(V.scalar_tensor_tensor(out=x, in0=x, scalar=s[:, 24:25], in1=BCf[0:n, 0:D],
                                              op0=ALU.subtract, op1=ALU.mult))
                    go(V.scalar_tensor_tensor(out=x, in0=x, scalar=s[:, 28:29], in1=BCf[0:n, D:2 * D],
                                              op0=ALU.mult, op1=ALU.add))
                    go(*[V.bn_stats(s[:, 6 * c:6 * c + 6], x[:, 512 * c:512 * c + 512]) for c in range(4)])
                    go(V.bn_aggr(s[:, 24:26], s[:, 0:24].rearrange("p (c s) -> p c s", c=4)))
                    V.tensor_scalar(s[:, 26:27], s[:, 25:26], EPS, None, ALU.add).then_inc(S("ln_var"), 1)

                def scale2(b, n, dst, scale):
                    dve.wait_ge(S("ex_ready"), 16)
                    dve_chain.tick(V.scalar_tensor_tensor(out=dst, in0=X[0:n, b, :], scalar=st[0:n, b, 24:25], in1=scale,
                                                          op0=ALU.subtract, op1=ALU.mult))

                def shift2(b, n, src, shift):
                    dve.wait_ge(S("ln_std"), LN_DONE["ln0"] + b + 1)
                    go(V.reciprocal(st[0:n, b, 28:29], st[0:n, b, 27:28]))
                    V.scalar_tensor_tensor(out=H[0:n, b, :], in0=src, scalar=st[0:n, b, 28:29], in1=shift,
                                           op0=ALU.mult, op1=ALU.add).then_inc(S("h2_ready"), 1)

                ln1(0, P)
                ln1(1, P)
                scale2(1, P, tmpO, H[:, 0, :])
                scale2(0, P, H[:, 0, :], H[:, 0, :])
                shift2(0, P, H[:, 0, :], H[:, 1, :])
                shift2(1, P, tmpO, H[:, 1, :])
                ln1(2, NS)
                scale2(2, NS, H[0:NS, 2, :], H[0:NS, 2, :])
                shift2(2, NS, H[0:NS, 2, :], shS)

                dve.wait_ge(S("rw_ready"), 2)
                dve.wait_ge(S("lg_ps"), 1)
                go(*[V.tensor_tensor(LG[0:n, b, :], bank[0:n, 2, 36 * b:36 * b + 36], rbias[0:n, :], ALU.add)
                     for b, n in BLK])
                KC4 = spread_mid(rc[:, R_K:R_K + 4], 3)
                KC8 = spread_mid(rc[:, R_K:R_K + 8], 3)

                def first_max(l, m, eq, key):
                    n = l.shape[-1]
                    go(V.tensor_reduce(m, l, AX.X, ALU.max))
                    go(V.tensor_tensor(eq, l, m.to_broadcast([P, 3, n]), ALU.is_equal))
                    go(V.tensor_tensor(eq, eq, key, ALU.mult))
                    go(V.tensor_reduce(rsm[:, 7, :, 0:1], eq, AX.X, ALU.max))
                    go(V.tensor_tensor(eq, eq, rsm[:, 7, :, 0:1].to_broadcast([P, 3, n]), ALU.is_equal))

                lg, le = LG[:, :, 0:NEG], LG[:, :, NEG:]
                gm, goh = rsm[:, 0, :, 0:1], RT[:, 0, :, 0:NEG]
                first_max(lg, gm, goh, KC4)
                V.tensor_tensor(rsm[:, 1, :, :], lg, gm.to_broadcast([P, 3, NEG]), ALU.subtract).then_inc(S("lg_sub"), 1)
                gsel = RT[:, 1, :, :].rearrange("p b (g e) -> p b g e", g=NEG)
                goh8 = spread(goh, EPG)
                go(V.tensor_tensor(gsel, le.rearrange("p b (g e) -> p b g e", g=NEG), goh8, ALU.mult))
                ein = RT[:, 2, :, 0:EPG]
                go(V.tensor_tensor(ein, gsel[:, :, 0, :], gsel[:, :, 1, :], ALU.add))
                go(V.tensor_tensor(ein, ein, gsel[:, :, 2, :], ALU.add))
                go(V.tensor_tensor(ein, ein, gsel[:, :, 3, :], ALU.add))
                m1, m2, o1, o2 = rsm[:, 2, :, 0:1], rsm[:, 3, :, 0:1], RT[:, 3, :, 0:EPG], RT[:, 4, :, 0:EPG]
                first_max(ein, m1, o1, KC8)
                go(V.scalar_tensor_tensor(out=RT[:, 5, :, 0:EPG], in0=o1, scalar=-BIG, in1=ein, op0=ALU.mult, op1=ALU.add))
                first_max(RT[:, 5, :, 0:EPG], m2, o2, KC8)
                V.tensor_tensor(m2, m2, m1, ALU.subtract).then_inc(S("lg_sub"), 1)
                dve.wait_ge(S("lg_exp"), 2)
                gv = rsm[:, 4, :, 0:1]
                go(V.tensor_reduce(gv, rsm[:, 1, :, :], AX.X, ALU.add))
                go(V.reciprocal(gv, gv), V.tensor_scalar(rsm[:, 5, :, 0:1], m2, 1.0, None, ALU.add))
                go(V.reciprocal(rsm[:, 5, :, 0:1], rsm[:, 5, :, 0:1]))
                go(V.tensor_tensor(cwt[:, :, 0:1], gv, rsm[:, 5, :, 0:1], ALU.mult))
                go(V.tensor_tensor(cwt[:, :, 1:2], cwt[:, :, 0:1], m2, ALU.mult))
                go(V.tensor_tensor(goh, goh, rc[:, R_VAL:R_VAL + 3].unsqueeze(2).to_broadcast([P, 3, NEG]), ALU.mult))
                M1, M2, M = RT[:, 6, :, :], RT[:, 7, :, :], RT[:, 8, :, :]
                go(*[V.tensor_tensor(Mx.rearrange("p b (g e) -> p b g e", g=NEG), goh8,
                                     ox.unsqueeze(2).to_broadcast([P, 3, NEG, EPG]), ALU.mult)
                     for Mx, ox in ((M1, o1), (M2, o2))])
                V.tensor_tensor(M, M1, M2, ALU.add).then_inc(S("m_ready"), 1)
                dve.wait_ge(S("rk_ps"), 1)
                go(V.tensor_copy(RK, bank[:, 3, 0:128].rearrange("p (b e) -> p b e", b=4)))
                rank, base = RK[:, 0:3, :], RT[:, 9, :, :]
                xe, inc, first_of, end_of = (xt[:, i, :] for i in range(4))
                go(V.tensor_scalar(xe, RK[:, 3, :], SLOTS + 1.0, None, ALU.is_ge))
                for k in range(2, T // SLOTS + 1):
                    go(V.scalar_tensor_tensor(out=xe, in0=RK[:, 3, :], scalar=SLOTS * k + 1.0, in1=xe,
                                              op0=ALU.is_ge, op1=ALU.add))
                go(V.tensor_tensor_scan(inc, ones[:, 0:E], xe, 0.0, ALU.mult, ALU.add))
                go(V.tensor_tensor(end_of, inc, rc[:, R_E:R_E + E], ALU.add))
                go(V.tensor_tensor(first_of, end_of, xe, ALU.subtract), V.tensor_scalar(end_of, end_of, 1.0, None, ALU.add))
                go(V.scalar_tensor_tensor(out=base, in0=spread_mid(first_of, 3), scalar=float(SLOTS), in1=rank,
                                          op0=ALU.mult, op1=ALU.add))
                go(V.tensor_tensor(M1, M1, base, ALU.mult), V.tensor_tensor(M2, M2, base, ALU.mult))
                go(V.tensor_reduce(slot_f[:, :, 0:1], M1, AX.X, ALU.add), V.tensor_reduce(slot_f[:, :, 1:2], M2, AX.X, ALU.add))
                go(V.tensor_copy(slot_i[:, :, :], slot_f[:, :, :]),
                   V.tensor_tensor(RQ[0:1, :, :], spread_mid(end_of[0:1, :], NBLK), spread(rc[0:1, R_J:R_J + NBLK], E),
                                   ALU.is_le))
                go(V.tensor_reduce(xf[0:1, :].unsqueeze(2), RQ[0:1, :, :], AX.X, ALU.add),
                   V.scalar_tensor_tensor(out=slot_f[:, :, :], in0=spread(rc[:, R_OUT:R_OUT + 3], 2), scalar=-1e6,
                                          in1=slot_f[:, :, :], op0=ALU.mult, op1=ALU.add))
                go(V.tensor_scalar(xf[0:1, :], xf[0:1, :], E - 1.0, None, ALU.min))
                go(V.tensor_copy(rint[0:1, 0:1], inc[0:1, E - 1:E]),
                   V.tensor_copy(rint[0:1, I_EXPERT:I_EXPERT + NBLK], xf[0:1, :]),
                   V.tensor_copy(rint[0:1, I_FIRST:I_FIRST + E], first_of[0:1, :]))

            @block.tensor
            def _(pe):
                pe.wait_ge(S("z_ready"), 1)
                for i in range(4):
                    w = arrived(pe, first[("glu", i, 0)]).rearrange("p (m n) -> p m n", m=2)
                    for m in range(8):
                        for k in range(2):
                            mm = pe.matmul(bank[:, m, 0:T], w[:, k, P * m:P * m + P], UT[:, 2 * i + k, :],
                                           start=(i == 0 and k == 0), stop=(i == 3 and k == 1))
                    mm.then_inc(used, 1)

                def project(h, i):
                    w = arrived(pe, first[("out", h, i)]).rearrange("p (m n) -> p m n", m=2)
                    for k in range(2):
                        for b in range(2):
                            for c in range(2):
                                pe.matmul(bank[:, OUT_BANKS[h][b][c], :], MT[:, 2 * i + k, P * b:P * b + P],
                                          w[:, k, 512 * c:512 * c + 512],
                                          start=(i == 0 and k == 0), stop=(i == 7 and k == 1))
                    for j in range(4):
                        k, c = j // 2, j % 2
                        mm = pe.matmul(bank[32 * j:32 * j + 32, OUT_BANKS[h][2], :], MT[:, 2 * i + k, SEQ:T],
                                       w[:, k, 512 * c:512 * c + 512], start=(i == 0), stop=(i == 7))
                    mm.then_inc(used, 1)

                pe.wait_ge(S("glu_sig"), 8)
                for i in range(4):
                    project(0, i)
                    for x in (2 * i, 2 * i + 1):
                        g, n0, n = x % 4, (0, P)[x // 4], (P, NS)[x // 4]
                        if x >= 2:
                            pe.wait_ge(S("gx_ready"), x - 1)
                        pe.matmul(bank[0:n, 6 + x % 2, :], con[32 * g:32 * g + 32, C_SEL + n0:C_SEL + n0 + n],
                                  MOD[32 * g:32 * g + 32, 0, :], start=True, stop=True).then_inc(S("gx_ps"), 1)
                for m in range(8):
                    pe.wait_ge(S("sq_ready"), m + 1)
                    mm = pe.matmul(bank[:, 5, 0:T], ones, sq[:, m, :], start=(m == 0), stop=(m == 7))
                mm.then_inc(S("rs_ps"), 1)
                for i in range(4, 8):
                    pe.wait_ge(S("ssmn_ready"), 2 * i - 6)
                    project(0, i)
                pe.wait_ge(S("gx_ready"), 8)
                pe.wait_ge(S("out_free"), 4)
                pe.wait_ge(S("smp_ready"), 4)
                for i in range(8):
                    project(1, i)
                    if i == 0:
                        pe.wait_ge(S("scale2_one"), 1)
                    for x in (2 * i, 2 * i + 1):
                        v, n0, n, _, g = EXPAND[x]
                        if x >= 3:
                            pe.wait_ge(S("ex_ready"), x - 2)
                        r = slice(32 * g, 32 * g + 32)
                        pe.matmul(bank[0:n, 2 + x % 3, :], con[r, C_SEL + n0:C_SEL + n0 + n], MOD[r, v, :],
                                  start=True, stop=True).then_inc(S("ex_ps"), 1)
                pe.wait_ge(S("out_free"), 8)
                pe.wait_ge(S("smp_ready"), 8)

                def transposes(b, n):
                    pe.wait_ge(S("h2_ready"), b + 1)
                    for i in range(4 * b, 4 * b + 4):
                        if i >= 2:
                            pe.wait_ge(S("h2t_ready"), i - 1)
                        for k in range(4):
                            kk = 4 * (i % 4) + k
                            mm = pe.transpose(bank[:, i % 2, n * k:n * k + n], H[0:n, b, kk:D:KD], ident[0:n, 0:n])
                        mm.then_inc(S("h2t_ps"), 1)

                def logits(b, n):
                    pe.wait_ge(S("h2t_ready"), 4 * b + 4)
                    for k in range(KD):
                        mm = pe.matmul(bank[0:n, 2, 36 * b:36 * b + 36], MT[:, k, P * b:P * b + n], rw[:, k, :],
                                       start=(k == 0), stop=(k == KD - 1))
                    return mm

                pe.wait_ge(S("rw_ready"), 2)
                transposes(0, P)
                transposes(1, P)
                logits(0, P)
                logits(1, P)
                transposes(2, NS)
                logits(2, NS).then_inc(S("lg_ps"), 1)
                pe.wait_ge(S("lg_ps"), 1)

                def gate2(i):
                    g, (n0, n) = i % 4, ((0, P), (P, NS))[i // 4]
                    if i >= 6:
                        pe.wait_ge(S("g2_ready"), i - 5)
                    r = slice(32 * g, 32 * g + 32)
                    pe.matmul(bank[0:n, G2_BANKS[i], :], con[r, C_SEL + n0:C_SEL + n0 + n], MOD[r, 3, :],
                              start=True, stop=True).then_inc(S("g2_ps"), 1)

                for i in range(6):
                    gate2(i)
                pe.wait_ge(S("m_ready"), 1)
                LT = rc[:, R_LT:R_LT + P]
                for b in range(4):
                    terms = [(ones, j) for j in range(min(b, 3))] + ([(LT, b)] if b < 3 else [])
                    for i, (w, j) in enumerate(terms):
                        mm = pe.matmul(bank[:, 3, 32 * b:32 * b + 32], w, RT[:, 8, j, :],
                                       start=(i == 0), stop=(i == len(terms) - 1))
                mm.then_inc(S("rk_ps"), 1)
                gate2(6)
                gate2(7)
                pe.wait_ge(S("g2_ready"), 4)
                for i in range(WARM):
                    pe.matmul(bank[:, 7, :], ones, H[:, 0, 0:512], start=True, stop=True)

        xT = BCf[:, 0:1024].rearrange("p (k s) -> p k s", k=KD)
        SG = BCf[:, 1024:1536]
        AC = BCf[:, 1536:2048]
        aT = BCf[:, 2048:2304].rearrange("p (j s) -> p j s", j=4)
        sel = BCf[:, 2304:2496].rearrange("p (b s) -> p b s", b=3)
        YS = BCf[:, 2560:3584].rearrange("p (j n) -> p j n", j=2)
        hi = slice(64, 128)

        def expert_loops(eng, body):
            with eng.Fori(0, E) as it:
                body(it)
            extra = eng.value_load(rint[0:1, 0:1], min_val=0, max_val=XB)
            with eng.Fori(E, NBLK) as it:
                with eng.If(extra > it - E):
                    body(it)
                    eng.nop()
                eng.nop()
            eng.nop()
            return extra

        with nc.Block() as block:
            @block.sync
            def _(sp):
                for j in range(PRE_RING + 3, RING):
                    load_expert_chunk(sp, 0, j)

                with sp.Fori(1, E) as e:
                    first = sp.value_load(rint[0:1, bass.ds(e + I_FIRST, 1)], min_val=1, max_val=NBLK - 1)
                    for j in range(RING):
                        sp.wait_ge(used, len(plan) + (first - 1) * RING + j + 1)
                        load_expert_chunk(sp, e, j)

            @block.vector
            def _(dve):
                V = nc.vector

                def select(it):
                    for b, n in BLK:
                        V.tensor_scalar(sel[:, b, :], con[:, C_IOTA:C_IOTA + SLOTS], slot_f[:, b, 0:1], None,
                                        ALU.is_equal).then_inc(S("sel_self"), 1)
                    dve.wait_ge(S("sel_self"), 6 * it + 3)
                    for b, n in BLK:
                        V.scalar_tensor_tensor(out=sel[:, b, :], in0=con[:, C_IOTA:C_IOTA + SLOTS],
                                               scalar=slot_f[:, b, 1:2], in1=sel[:, b, :],
                                               op0=ALU.is_equal, op1=ALU.add).then_inc(S("sel_self"), 1)
                    dve.wait_ge(S("sel_self"), 6 * it + 6)
                    V.tensor_scalar(slot_f[:, :, :], slot_f[:, :, :], float(SLOTS), None, ALU.subtract)\
                     .then_inc(S("sel_ready"), 1)
                    dve.wait_ge(S("sel_ready"), it + 1)

                def body(e):
                    dve.wait_ge(S("sg_ready"), e + 1)
                    V.tensor_tensor(AC[hi, :], SG[hi, :], bank[hi, 2, :], ALU.mult).then_inc(S("act_ready"), 1)
                    dve.wait_ge(S("xg_ps"), e + 2)
                    V.tensor_copy(xT[:, 8:16, :], bank[:, 1, :].rearrange("p (k s) -> p k s", k=8)).then_inc(S("xg_ready"), 1)
                    select(e + 2)
                    dve.wait_ge(used, len(plan) + (e + 1) * RING)
                    dve.wait_ge(S("y_written"), 32 * e + 32)
                    V.tensor_copy(YS[:, 1, :], bank[:, 5, :]).then_inc(S("ys_dve"), 1)

                dve.nop().then_inc(S("ys_dve"), 1)
                select(0)
                dve.wait_ge(S("xg_ps"), 1)
                V.tensor_copy(xT[:, 8:16, :], bank[:, 1, :].rearrange("p (k s) -> p k s", k=8)).then_inc(S("xg_ready"), 1)
                select(1)
                expert_loops(dve, body)

            @block.scalar
            def _(act):
                def body(e):
                    act.wait_ge(used, len(plan) + e * RING + 8)
                    nc.scalar.activation(SG[hi, :], bank[0:64, 2, :], ACT.Silu).then_inc(S("sg_ready"), 1)
                    act.wait_ge(S("xg_ps"), e + 2)
                    nc.scalar.copy(xT[:, 0:8, :], bank[:, 0, :].rearrange("p (k s) -> p k s", k=8)).then_inc(S("xg_ready"), 1)
                    act.wait_ge(S("at_ps"), e + 1)
                    nc.scalar.copy(aT, bank[:, 3, 0:256].rearrange("p (j s) -> p j s", j=4)).then_inc(S("at_ready"), 1)
                    act.wait_ge(used, len(plan) + (e + 1) * RING)
                    act.wait_ge(S("y_written"), 32 * e + 32)
                    nc.scalar.copy(YS[:, 0, :], bank[:, 4, :]).then_inc(S("ys_act"), 1)
                    act.wait_ge(S("ys_act"), e + 2)
                    act.wait_ge(S("ys_dve"), e + 2)
                    for c in range(2):
                        act.dma_start(y_dram[bass.ds(e * SLOTS, SLOTS), :].rearrange("s (j c n) -> c s j n", j=2, c=2)[c],
                                      YS[64 * c:64 * c + 64, :, :]).then_inc(S("y_written"), 16)

                act.nop().then_inc(S("ys_act"), 1)
                act.nop().then_inc(S("y_written"), 32)
                act.wait_ge(S("xg_ps"), 1)
                nc.scalar.copy(xT[:, 0:8, :], bank[:, 0, :].rearrange("p (k s) -> p k s", k=8)).then_inc(S("xg_ready"), 1)
                extra = expert_loops(act, body)
                act.wait_ge(S("y_written"), 32 * (extra + E) + 32)
                nc.scalar.activation(st[:, 0, 29:30], st[:, 0, 28:29], ACT.Sqrt)
                act.nop()

            @block.tensor
            def _(pe):
                def gather(it):
                    pe.wait_ge(S("sel_ready"), it + 1)
                    for k in range(KD):
                        for b, n in BLK:
                            mm = pe.matmul(bank[:, k // 8, SLOTS * (k % 8):SLOTS * (k % 8) + SLOTS], H[:, b, k:D:KD],
                                           sel[:, b, :], start=(b == 0), stop=(b == 2))
                    mm.then_inc(S("xg_ps"), 1)

                def body(e):
                    expert = pe.value_load(rint[0:1, bass.ds(e + I_EXPERT, 1)], min_val=0, max_val=E - 1)
                    pe.wait_ge(S("xg_ready"), 2 * e + 2)
                    for k in range(KD):
                        for i in range(2):
                            j = 2 * (k // 4) + i
                            if k % 4 == 0:
                                pe.wait_ge(landed[j], 16 * (last_slot_uses[j] + 1) + 16 * expert)
                            mm = pe.matmul(bank[64 * i:64 * i + 64, 2, :], xT[:, k, :],
                                           ring[:, j, 512 * (k % 4):512 * (k % 4) + 512], start=(k == 0), stop=(k == KD - 1))
                            if k % 4 == 3:
                                mm.then_inc(used, 1)
                    gather(e + 1)
                    pe.wait_ge(S("act_ready"), e + 1)
                    for j in range(4):
                        mm = pe.matmul(bank[:, 3, SLOTS * j:SLOTS * j + SLOTS], AC[hi, j:FE:4], ident[hi, 64:128],
                                       start=True, stop=True)
                    mm.then_inc(S("at_ps"), 1)
                    pe.wait_ge(S("at_ready"), e + 1)
                    pe.wait_ge(S("ys_act"), e + 1)
                    pe.wait_ge(S("ys_dve"), e + 1)
                    for j in range(4):
                        pe.wait_ge(landed[8 + j], 16 * (last_slot_uses[8 + j] + 1) + 16 * expert)
                        for c in range(4):
                            mm = pe.matmul(bank[64 * (c % 2):64 * (c % 2) + 64, 4 + c // 2, :], aT[:, j, :],
                                           ring[:, 8 + j, 512 * c:512 * c + 512], start=(j == 0), stop=(j == 3))
                        mm.then_inc(used, 1)

                gather(0)
                expert_loops(pe, body)

        Y = ring[:, 0:6, :].rearrange("p (b i) d -> p b i d", i=2)
        F_ORDER = [(2, NS), (0, P), (1, P)]
        Y_NTH, LN_NTH = {2: 1, 0: 2, 1: 3}, {0: 1, 2: 2, 1: 3}
        with nc.Block() as block:
            @block.gpsimd
            def _(pool):
                for b, n in F_ORDER:
                    for i in range(2):
                        pool.indirect_dma_start(Y[0:n, b, i, :], None, y_dram[:, :],
                                                bass.IndirectOffsetOnAxis(ap=slot_i[0:n, b, i:i + 1], axis=0))\
                            .then_inc(S(f"y_in{b}"), 16)
                pool.wait_ge(S("y_sum"), Y_NTH[2])
                nc.gpsimd.tensor_tensor(Y[0:NS, 2, 0, :], Y[0:NS, 2, 0, :], G2[0:NS, 1, :], ALU.mult).then_inc(S("smp_gated"), 1)
                pool.wait_ge(S("ln2_in"), 32)
                for b, n in ((0, P), (2, NS)):
                    pool.wait_ge(S("normed"), LN_NTH[b])
                    nc.gpsimd.tensor_tensor(X[0:n, b, :], X[0:n, b, :], GE[0:n, 1, :], ALU.add).then_inc(S("x_out"), 1)

            @block.sync
            def _(sp):
                sp.wait_ge(S("x_out"), LN_NTH[0])
                sp.dma_start(o["y_prompt"][0, 0:P, :], X[:, 0, :]).then_inc(S("out_done"), 16)
                sp.wait_ge(S("x_out"), LN_NTH[2])
                sp.dma_start(o["y_sample"].rearrange("b t d -> (b t) d"), X[0:NS, 2, :]).then_inc(S("out_done"), 16)
                for h in range(2):
                    c = slice(h * D // 2, (h + 1) * D // 2)
                    sp.wait_ge(S("x_out1"), h + 1)
                    sp.dma_start(o["y_prompt"][0, P:2 * P, c], X[:, 1, c]).then_inc(S("out_done"), 16)
                sp.wait_ge(S("out_done"), 64)

            @block.scalar
            def _(act):
                def weigh(b, n):
                    act.wait_ge(S(f"y_in{b}"), 32)
                    nc.scalar.mul(Y[0:n, b, 0, :], Y[0:n, b, 0, :], cwt[0:n, b, 0:1]).then_inc(S("y_weighed"), 1)

                def root(b, n):
                    act.wait_ge(S("ln_var"), LN_DONE["ln2"] + LN_NTH[b])
                    nc.scalar.activation(st[0:n, b, 27:28], st[0:n, b, 26:27], ACT.Sqrt).then_inc(S("ln_std"), 1)

                weigh(2, NS), weigh(0, P), root(0, P), weigh(1, P), root(2, NS), root(1, P)

            @block.vector
            def _(dve):
                V = nc.vector

                def go(i):
                    dve_chain.tick(i)
                    dve_chain.settle(dve)

                def both(b, n):
                    dve.wait_ge(S("y_weighed"), Y_NTH[b])
                    V.scalar_tensor_tensor(out=Y[0:n, b, 0, :], in0=Y[0:n, b, 1, :], scalar=cwt[0:n, b, 1:2],
                                           in1=Y[0:n, b, 0, :], op0=ALU.mult, op1=ALU.add).then_inc(S("y_sum"), 1)

                def gate(b):
                    dve.wait_ge(S("y_sum"), Y_NTH[b])
                    V.tensor_tensor(Y[:, b, 0, :], Y[:, b, 0, :], G2[:, 0, :], ALU.mult).then_inc(S("gated"), 1)

                def residual(b, n):
                    s, x = st[0:n, b, :], X[0:n, b, :]
                    if b == 2:
                        dve.wait_ge(S("smp_gated"), 3)
                    else:
                        dve.wait_ge(S("gated"), b + 1)
                    go(V.scalar_tensor_tensor(out=x, in0=x, scalar=ALPHA, in1=Y[0:n, b, 0, :], op0=ALU.mult, op1=ALU.add))
                    for c in range(4):
                        dve_chain.tick(V.bn_stats(s[:, 6 * c:6 * c + 6], x[:, 512 * c:512 * c + 512]))
                    dve_chain.settle(dve)
                    go(V.bn_aggr(s[:, 24:26], s[:, 0:24].rearrange("p (c s) -> p c s", c=4)))
                    V.tensor_scalar(s[:, 26:27], s[:, 25:26], EPS, None, ALU.add).then_inc(S("ln_var"), 1)

                def norm(b, n, add):
                    s, x = st[0:n, b, :], X[0:n, b, :]
                    dve.wait_ge(S("ln_std"), LN_DONE["ln2"] + LN_NTH[b])
                    go(V.reciprocal(s[:, 28:29], s[:, 27:28]))
                    dve.wait_ge(S("ln2_in"), 32)
                    if add:
                        for h in range(2):
                            c = slice(h * D // 2, (h + 1) * D // 2)
                            go(V.scalar_tensor_tensor(out=x[:, c], in0=x[:, c], scalar=s[:, 24:25], in1=GE[0:n, 0, c],
                                                      op0=ALU.subtract, op1=ALU.mult))
                            V.scalar_tensor_tensor(out=x[:, c], in0=x[:, c], scalar=s[:, 28:29], in1=GE[0:n, 1, c],
                                                   op0=ALU.mult, op1=ALU.add).then_inc(S("x_out1"), 1)
                    else:
                        go(V.tensor_scalar(x, x, s[:, 24:25], s[:, 28:29], ALU.subtract, ALU.mult))
                        V.tensor_tensor(x, x, GE[0:n, 0, :], ALU.mult).then_inc(S("normed"), 1)

                both(2, NS)
                both(0, P)
                gate(0)
                residual(0, P)
                residual(2, NS)
                norm(0, P, False)
                norm(2, NS, False)
                both(1, P)
                gate(1)
                residual(1, P)
                norm(1, P, True)


_OUTS = [("y_prompt", (1, SEQ, D)), ("y_sample", (NB, DS, D)),
         ("k_win_prompt", (1, 1, WIN, NKV, HD)), ("v_win_prompt", (1, 1, WIN, NKV, HD)),
         ("ssm_re_prompt", (1, 1, G, ST)), ("ssm_im_prompt", (1, 1, G, ST)),
         ("k_win_sample", (1, NB, WIN, NKV, HD)), ("v_win_sample", (1, NB, WIN, NKV, HD)),
         ("ssm_re_sample", (1, NB, G, ST)), ("ssm_im_sample", (1, NB, G, ST))]


def kernel(**inputs):
    import concourse.bacc as bacc
    from concourse.bass_utils import run_bass_kernel_spmd

    nc = bacc.Bacc("TRN2", target_bir_lowering=False, num_devices=1)
    arrays = {f"in_{k}": np.ascontiguousarray(v) for k, v in inputs.items()}
    arrays["in_consts"], arrays["in_masks"], arrays["in_route_consts"] = constants()
    a = {k[3:]: nc.dram_tensor(k, v.shape, mybir.dt.from_np(v.dtype), kind="ExternalInput").ap()
         for k, v in arrays.items()}
    o = {k: nc.dram_tensor(f"out_{k}", s, F32, kind="ExternalOutput").ap() for k, s in _OUTS}
    scratch = (nc.dram_tensor("attn_dram", (NS, DA), F32, kind="Internal").ap(),
               nc.dram_tensor("y_dram", (NBLK * SLOTS, D), F32, kind="Internal").ap())
    build(nc, a, o, scratch)
    r = run_bass_kernel_spmd(nc, [arrays], core_ids=[0])
    return tuple(r.results[0][f"out_{k}"] for k, _ in _OUTS)
```
